# Optimizing a Trainium2 kernel written in Bass

```python
import jax, jax.numpy as jnp
from jax import lax
import numpy as np

D_MODEL = 1024
BATCH = 1
SEQ = 512
DEPTH = 1
DEC_BATCH = 8
DEC_SEQ = 16
PAST_LEN = 256

CHUNK = 64
N_META = 16
M_HEADS = 4
D_M = D_MODEL
M_HEAD_DIM = D_M // M_HEADS
D_C = D_MODEL
CONV_W = 31
D_FF = 4 * D_MODEL
EPS = 1e-6

OFF_Q = 0
OFF_K = OFF_Q + D_M
OFF_V = OFF_K + D_M
OFF_O = OFF_V + D_M
OFF_I = OFF_O + D_M
OFF_F = OFF_I + M_HEADS
OFF_CA = OFF_F + M_HEADS
OFF_CB = OFF_CA + D_C
OFF_GM = OFF_CB + D_C
OFF_GC = OFF_GM + D_MODEL
N_IN = OFF_GC + D_MODEL

kernel_name = "mlstm_conformer_gated_stream_step"

def rmsnorm(x, g):
    xf = x.astype(jnp.float32)
    y = xf * lax.rsqrt(jnp.mean(xf * xf, axis=-1, keepdims=True) + EPS)
    return (y * g.astype(jnp.float32)).astype(x.dtype)

def layernorm(x, g, b):
    xf = x.astype(jnp.float32)
    mu = jnp.mean(xf, axis=-1, keepdims=True)
    xc = xf - mu
    y = xc * lax.rsqrt(jnp.mean(xc * xc, axis=-1, keepdims=True) + EPS)
    return (y * g.astype(jnp.float32) + b.astype(jnp.float32)).astype(x.dtype)

def mlstm_chunk(carry, blk):
    C0, n0, m0 = carry
    q, k, v, it, lf = blk
    L = q.shape[2]
    b = jnp.cumsum(lf, axis=-1)
    a = b + m0[..., None]
    causal = jnp.tril(jnp.ones((L, L), dtype=bool))
    dmat = jnp.where(causal, b[..., :, None] - b[..., None, :] + it[..., None, :], -jnp.inf)
    m = jnp.maximum(a, jnp.max(dmat, axis=-1))
    w_state = jnp.exp(a - m)
    w_intra = jnp.exp(dmat - m[..., None])
    p = w_intra * jnp.einsum('bhtd,bhsd->bhts', q, k)
    num = jnp.einsum('bhts,bhse->bhte', p, v) + w_state[..., None] * jnp.einsum('bhed,bhtd->bhte', C0, q)
    den = jnp.sum(p, axis=-1) + w_state * jnp.einsum('bhd,bhtd->bht', n0, q)
    h = num / jnp.maximum(jnp.abs(den), jnp.exp(-m))[..., None]
    m_last = m[..., -1]
    w_last = w_state[..., -1]
    ws = w_intra[..., -1, :]
    C1 = w_last[..., None, None] * C0 + jnp.einsum('bhs,bhse,bhsd->bhed', ws, v, k)
    n1 = w_last[..., None] * n0 + jnp.einsum('bhs,bhsd->bhd', ws, k)
    return (C1, n1, m_last), h

def mlstm_sequence(carry, blk, n_lead):
    if n_lead == 0:
        return mlstm_chunk(carry, blk)
    lead = tuple(t[:, :, :n_lead] for t in blk)
    carry, h_lead = mlstm_chunk(carry, lead)
    rest = tuple(t[:, :, n_lead:] for t in blk)
    n_chunks = rest[0].shape[2] // CHUNK

    def to_chunks(t):
        t = t.reshape(t.shape[:2] + (n_chunks, CHUNK) + t.shape[3:])
        return jnp.moveaxis(t, 2, 0)

    carry, h_rest = lax.scan(mlstm_chunk, carry, tuple(to_chunks(t) for t in rest))
    h_rest = jnp.moveaxis(h_rest, 0, 2)
    h_rest = h_rest.reshape(h_rest.shape[:2] + (n_chunks * CHUNK, M_HEAD_DIM))
    return carry, jnp.concatenate([h_lead, h_rest], axis=2)

def depthwise_conv_valid(padded, w, bias):
    y = lax.conv_general_dilated(padded, w[:, None, :].astype(padded.dtype), window_strides=(1,),
                                 padding='VALID', dimension_numbers=('NWC', 'WIO', 'NWC'),
                                 feature_group_count=padded.shape[-1])
    return y + bias.astype(padded.dtype)

def layer(x, C0, n0, m0, conv_buf, n_lead, g_pre_mix, w_in, b_if, g_headnorm, w_branch_m,
          conv_w, conv_b, ln_g, ln_b, w_branch_c, w_out, g_post_mix, g_pre_ffn, w_ff1, w_ff2, g_post_ffn):
    B, L, _ = x.shape
    hin = rmsnorm(x, g_pre_mix)
    z = hin @ w_in.astype(hin.dtype)
    f32 = jnp.float32

    def heads(t):
        return t.reshape(B, L, M_HEADS, M_HEAD_DIM).transpose(0, 2, 1, 3).astype(f32)

    q = heads(z[..., OFF_Q:OFF_K])
    k = heads(z[..., OFF_K:OFF_V]) * (M_HEAD_DIM ** -0.5)
    v = heads(z[..., OFF_V:OFF_O])
    o_gate = jax.nn.sigmoid(z[..., OFF_O:OFF_I].astype(f32))
    bif = b_if.astype(f32)
    it = (z[..., OFF_I:OFF_F].astype(f32) + bif[:M_HEADS]).transpose(0, 2, 1)
    lf = jax.nn.log_sigmoid(z[..., OFF_F:OFF_CA].astype(f32) + bif[M_HEADS:]).transpose(0, 2, 1)
    carry = (C0.astype(f32), n0.astype(f32), m0.astype(f32))
    (C1, n1, m1), hm = mlstm_sequence(carry, (q, k, v, it, lf), n_lead)
    mu = jnp.mean(hm, axis=-1, keepdims=True)
    hc = hm - mu
    hm = hc * lax.rsqrt(jnp.mean(hc * hc, axis=-1, keepdims=True) + EPS)
    hm = hm.transpose(0, 2, 1, 3).reshape(B, L, D_M) * g_headnorm.astype(f32) * o_gate
    branch_m = hm.astype(x.dtype) @ w_branch_m.astype(x.dtype)

    u = z[..., OFF_CA:OFF_CB] * jax.nn.sigmoid(z[..., OFF_CB:OFF_GM])
    padded = jnp.concatenate([conv_buf.astype(u.dtype), u], axis=1)
    new_buf = padded[:, -(CONV_W - 1):]
    cv = depthwise_conv_valid(padded, conv_w, conv_b)
    cv = jax.nn.silu(layernorm(cv, ln_g, ln_b))
    branch_c = cv @ w_branch_c.astype(cv.dtype)

    gm = jax.nn.sigmoid(z[..., OFF_GM:OFF_GC])
    gc = jax.nn.sigmoid(z[..., OFF_GC:N_IN])
    merged = gm * branch_m + gc * branch_c
    x = x + rmsnorm(merged @ w_out.astype(merged.dtype), g_post_mix)

    hf = rmsnorm(x, g_pre_ffn)
    hf = jnp.square(jax.nn.relu(hf @ w_ff1.astype(hf.dtype))) @ w_ff2.astype(hf.dtype)
    x = x + rmsnorm(hf, g_post_ffn)
    return x, C1, n1, m1, new_buf

def setup_inputs(seed: int = 0) -> dict:
    key = jax.random.key(seed)
    ks = jax.random.split(key, 24)
    f32 = jnp.float32
    nrm = lambda k, s, sc: jax.random.normal(k, s, f32) * sc
    gain = lambda k, s: 1.0 + 0.05 * jax.random.normal(k, s, f32)
    b_i = 0.1 * jax.random.normal(ks[20], (DEPTH, M_HEADS), f32)
    b_f = jnp.linspace(3.0, 6.0, M_HEADS, dtype=f32)[None, :] + 0.01 * jax.random.normal(ks[21], (DEPTH, M_HEADS), f32)
    return {
        "x_prompt": nrm(ks[0], (BATCH, SEQ, D_MODEL), 1.0),
        "x_sample": nrm(ks[1], (DEC_BATCH, DEC_SEQ, D_MODEL), 1.0),
        "state_mlstm_C": nrm(ks[2], (DEPTH, DEC_BATCH, M_HEADS, M_HEAD_DIM, M_HEAD_DIM), 0.05),
        "state_mlstm_n": nrm(ks[3], (DEPTH, DEC_BATCH, M_HEADS, M_HEAD_DIM), 0.1),
        "state_mlstm_m": nrm(ks[4], (DEPTH, DEC_BATCH, M_HEADS), 0.5),
        "cache_conv": nrm(ks[5], (DEPTH, DEC_BATCH, CONV_W - 1, D_C), 0.5),
        "meta_tokens": nrm(ks[6], (N_META, D_MODEL), 1.0),
        "g_pre_mix": gain(ks[7], (DEPTH, D_MODEL)),
        "w_in": nrm(ks[8], (DEPTH, D_MODEL, N_IN), D_MODEL ** -0.5),
        "b_if": jnp.concatenate([b_i, b_f], axis=-1),
        "g_headnorm": gain(ks[9], (DEPTH, D_M)),
        "w_branch_m": nrm(ks[10], (DEPTH, D_M, D_MODEL), D_M ** -0.5),
        "conv_w": nrm(ks[11], (DEPTH, CONV_W, D_C), CONV_W ** -0.5),
        "conv_b": nrm(ks[12], (DEPTH, D_C), 0.02),
        "ln_g": gain(ks[13], (DEPTH, D_C)),
        "ln_b": nrm(ks[14], (DEPTH, D_C), 0.02),
        "w_branch_c": nrm(ks[15], (DEPTH, D_C, D_MODEL), D_C ** -0.5),
        "w_out": nrm(ks[16], (DEPTH, D_MODEL, D_MODEL), D_MODEL ** -0.5),
        "g_post_mix": gain(ks[17], (DEPTH, D_MODEL)),
        "g_pre_ffn": gain(ks[18], (DEPTH, D_MODEL)),
        "w_ff1": nrm(ks[19], (DEPTH, D_MODEL, D_FF), D_MODEL ** -0.5),
        "w_ff2": nrm(ks[22], (DEPTH, D_FF, D_MODEL), D_FF ** -0.5),
        "g_post_ffn": gain(ks[23], (DEPTH, D_MODEL)),
    }

def reference(x_prompt, x_sample, state_mlstm_C, state_mlstm_n, state_mlstm_m, cache_conv,
              meta_tokens, g_pre_mix, w_in, b_if, g_headnorm, w_branch_m, conv_w, conv_b,
              ln_g, ln_b, w_branch_c, w_out, g_post_mix, g_pre_ffn, w_ff1, w_ff2, g_post_ffn):
    f32 = jnp.float32
    B = x_prompt.shape[0]
    xp = jnp.concatenate([jnp.broadcast_to(meta_tokens.astype(x_prompt.dtype)[None], (B, N_META, D_MODEL)),
                          x_prompt], axis=1)
    xs = x_sample
    Cp, np_, mp, bp = [], [], [], []
    Cs, ns, ms, bs = [], [], [], []
    for l in range(DEPTH):
        w = (g_pre_mix[l], w_in[l], b_if[l], g_headnorm[l], w_branch_m[l], conv_w[l], conv_b[l],
             ln_g[l], ln_b[l], w_branch_c[l], w_out[l], g_post_mix[l], g_pre_ffn[l], w_ff1[l], w_ff2[l],
             g_post_ffn[l])
        zC = jnp.zeros((B, M_HEADS, M_HEAD_DIM, M_HEAD_DIM), f32)
        zn = jnp.zeros((B, M_HEADS, M_HEAD_DIM), f32)
        zm = jnp.zeros((B, M_HEADS), f32)
        zb = jnp.zeros((B, CONV_W - 1, D_C), xp.dtype)
        xp, c1, n1, m1, b1 = layer(xp, zC, zn, zm, zb, N_META, *w)
        Cp.append(c1); np_.append(n1); mp.append(m1); bp.append(b1)
        xs, c2, n2, m2, b2 = layer(xs, state_mlstm_C[l], state_mlstm_n[l], state_mlstm_m[l], cache_conv[l], 0, *w)
        Cs.append(c2); ns.append(n2); ms.append(m2); bs.append(b2)
    y_prompt = xp[:, N_META:]
    y_sample = xs
    C_prompt = jnp.stack(Cp); n_prompt = jnp.stack(np_); m_prompt = jnp.stack(mp); conv_prompt = jnp.stack(bp)
    C_sample = jnp.stack(Cs); n_sample = jnp.stack(ns); m_sample = jnp.stack(ms); conv_sample = jnp.stack(bs)
    return (y_prompt, y_sample, C_prompt, n_prompt, m_prompt, conv_prompt, C_sample, n_sample, m_sample, conv_sample)


_drawn_inputs = setup_inputs


def setup_inputs(seed=0):
    import zlib

    import numpy as np

    out = dict(_drawn_inputs(seed))
    spreads = {}
    factors = {'ln_b': 5.038}
    for name, (base, spread) in spreads.items():
        noise = np.random.default_rng([zlib.crc32(name.encode()), seed]).standard_normal(out[name].shape)
        drawn = base * np.exp(spread * noise) if base else spread * noise
        out[name] = __import__('jax').numpy.asarray(drawn.astype(out[name].dtype))
    for name, factor in factors.items():
        out[name] = (out[name] * factor).astype(out[name].dtype)
    return out
```

```python
import numpy as np
import concourse.bass as bass
from concourse import mybir

F32 = mybir.dt.float32
R32 = mybir.dt.float32r
ALU = mybir.AluOpType
ACT = mybir.ActivationFunctionType

D = 1024
P = 128
KT = D // P
HEADS, DH = 4, 256
CONV_W = 31
PAD = CONV_W - 1
DFF = 4 * D
NMETA, SEQ = 16, 512
NB, LB = 8, 16
EPS = 1e-6
OFF_Q, OFF_K, OFF_V, OFF_O = 0, D, 2 * D, 3 * D
OFF_I = 4 * D
OFF_CA = OFF_I + 2 * HEADS
OFF_CB, OFF_GM, OFF_GC = OFF_CA + D, OFF_CA + 2 * D, OFF_CA + 3 * D
N_IN = OFF_GC + D

TS = NB * LB
TP = NMETA + SEQ
T = TS + TP
HALF = T // 2
NEG = -1e30
CHUNKS = [(TS, NMETA)] + [(TS + NMETA + P * c, P) for c in range(SEQ // P)] + [(0, TS)]
NPC = 5
SMP = 5

PER_HEAD = 12
N_HEADS0 = 1
N_GM0 = N_HEADS0 + PER_HEAD * HEADS
N_GC0 = N_GM0 + 2 * KT
N_OUT0 = N_GC0 + 2 * KT
N_FF0 = N_OUT0 + KT
NSTAGE = 4

S_SLOT = {0: 0, 2: 1, 4: 2, 6: 3, 8: 4, 10: 5}
NUM_SLOT = {1: 0, 3: 1, 5: 2, 7: 3, 9: 4, 13: 5}
UPD_SLOT = {0: 0, 2: 1, 4: 2, 6: 3, 8: 4, 10: 5, 11: 6, 12: 7}
TR_SLOT = {0: 0, 1: 1, 2: 2, 3: 3, 5: 4, 6: 5, 8: 6, 10: 7}
INT_SLOT = {1: 0, 2: 1, 3: 2, 4: 3, 6: 4, 7: 5, 9: 6, 11: 7}
NSLOT = 14
UPDATES = []
for _s in range(NSLOT):
    if _s in NUM_SLOT and NUM_SLOT[_s] < NPC:
        UPDATES.append(("U", NUM_SLOT[_s]))
    if _s in UPD_SLOT:
        UPDATES.append(("D", UPD_SLOT[_s]))
V_HEAD = 26
NUPD = len(UPDATES)
C0RING = 4
STORE_SLOT = {_s + 1: _b for _s, _b in UPD_SLOT.items()}
LOAD_SLOT = {_s + 2: _b + C0RING for _s, _b in UPD_SLOT.items() if _b + C0RING < NB}
CONV_TILE = {2: 7, 3: 6, 4: 6, 5: 6, 6: 6, 7: 5}
CONV_SLOT = {s: 3 if s % 2 else 2 for s in range(NSLOT) if 0 < s < 12}
TAPS = 2 * CONV_W
assert sum(CONV_TILE.values()) + sum(CONV_SLOT.values()) >= TAPS


def build(nc, a):
    def sb(name, shape, dt=F32):
        return nc.alloc_sbuf_tensor(name, shape, dt)

    XH, XL = sb("XH", [P, KT, T], R32), sb("XL", [P, KT, T], R32)
    GH, GL = sb("GH", [P, KT, T], R32), sb("GL", [P, KT, T], R32)
    CV = sb("CV", [P, KT, T])
    ST = sb("ST", [P, NSTAGE, KT, P])
    WH, WL = sb("WH", [P, 2, KT, P], R32), sb("WL", [P, 2, KT, P], R32)
    sizes = [("q", 2 * T), ("k", 2 * T), ("qw", 2 * T), ("vn", 6 * 257), ("so", 2 * T), ("kt", 6 * 256),
             ("vt", 6 * 257), ("vws", 2 * 257), ("c0", C0RING * 512), ("c0t", 512), ("hti", 256),
             ("pt", 2 * P), ("bc", 2 * T), ("ct", 2 * 257), ("up", 2 * (PAD + TP + NB * (PAD + LB)))]
    off, total = {}, 0
    for nm, n in sizes:
        off[nm] = total
        total += n
    WK = sb("WK", [P, total])

    def wk(o, n):
        return WK[:, o:o + n]

    q = wk(off["q"], 2 * T).rearrange("p (a t) -> p a t", a=2)
    k = wk(off["k"], 2 * T).rearrange("p (a t) -> p a t", a=2)
    qw = wk(off["qw"], 2 * T).rearrange("p (a t) -> p a t", a=2)
    vf = wk(off["vn"], 2 * T).rearrange("p (a t) -> p a t", a=2)
    num = wk(off["vn"], 6 * 257).rearrange("p (c e) -> p c e", c=6)
    so = wk(off["so"], 2 * T).rearrange("p (a t) -> p a t", a=2)
    ktok = wk(off["kt"], 6 * 256).rearrange("p (c e) -> p c e", c=6)
    vtok = wk(off["vt"], 6 * 257).rearrange("p (c e) -> p c e", c=6)
    vws = wk(off["vws"], 2 * 257).rearrange("p (c e) -> p c e", c=2)
    c0 = wk(off["c0"], C0RING * 512).rearrange("p (b i d) -> p b i d", b=C0RING, i=2)
    c0t = wk(off["c0t"], 512).rearrange("p (j e) -> p j e", j=2)
    hti = wk(off["hti"], 256).rearrange("p (i t) -> p i t", i=2)
    pt = wk(off["pt"], 2 * P).rearrange("p (b t) -> p b t", b=2)
    bcm, bcw = wk(off["bc"], T), wk(off["bc"] + T, T)
    ct = wk(off["ct"], 2 * 257).rearrange("p (j e) -> p j e", j=2)
    PL = PAD + TP
    UPN = PL + NB * (PAD + LB)
    up = wk(off["up"], 2 * UPN).rearrange("p (a t) -> p a t", a=2)
    ups = up[:, :, PL:UPN].rearrange("p a (b t) -> p a b t", b=NB)
    MG = wk(0, KT * T).rearrange("p (k t) -> p k t", k=KT)
    sg = wk(off["kt"], 2 * T).rearrange("p (a t) -> p a t", a=2)
    xtok0 = wk(0, 6 * D).rearrange("p (c e) -> p c e", c=6)
    xtok5 = wk(off["so"], 6 * D).rearrange("p (c e) -> p c e", c=6)
    nqs = wk(off["vn"] + SMP * 257, 2 * TS).rearrange("p (j t) -> p j t", j=2)
    ust = wk(off["vn"], 5 * 256)
    WIN = PAD + LB
    UR = WIN + PAD
    xc = wk(off["c0t"], KT * NB * PAD).rearrange("p (k w) -> p k w", k=KT)
    gcs = wk(off["vt"], KT * T).rearrange("p (k t) -> p k t", k=KT)
    assert off["c0t"] + KT * NB * PAD <= off["up"] and off["pt"] == off["hti"] + 256
    z0 = off["so"] + 6 * D
    assert z0 + 8 * T <= total
    tmp = [wk(z0 + i * T, T) for i in range(8)]
    ln = [wk(off["vt"] + KT * T + i * T, T) for i in range(5)]
    assert off["vt"] + KT * T + 5 * T <= total and off["vt"] - off["kt"] >= 2 * T

    ident, ones, onesd = sb("ident", [P, P]), sb("ones", [P, P]), sb("onesd", [P, 1])
    maskc, maskd, bmask = sb("maskc", [P, P]), sb("maskd", [P, P]), sb("bmask", [P, NB])
    prm = sb("prm", [P, 64])
    cwt = sb("cwt", [P, KT, CONV_W])
    CVF = CV[:, :, :].rearrange("p k t -> p (k t)")
    VEC = ["g_pre_mix", "g_headnorm", "conv_b", "ln_g", "ln_b", "g_post_mix", "g_pre_ffn", "g_post_ffn"]

    def vec(name, kk, n=1):
        o = VEC.index(name) * KT
        return prm[:, bass.ds(o + kk, n)] if not isinstance(kk, int) else prm[:, o + kk:o + kk + n]

    colA = sb("colA", [P, HEADS, 31])
    colH = sb("colH", [P, 31])
    cwu = sb("cwu", [P, 2, CONV_W + 1])
    ghd = sb("ghd", [P, 2])
    wlb = sb("wlb", [NB, HEADS])
    n0t = sb("n0t", [P, 2, NB * HEADS])
    n0b = sb("n0b", [NB, DH])
    wsb = sb("wsb", [P, NB])
    nsel = sb("nsel", [P, 2, NB])
    bst, mv = sb("bst", [P, 6, 6]), sb("mv", [P, 6, 2])
    sm = sb("sm", [P, 48])
    bif = sb("bif", [2 * HEADS, 1])
    mhalf = sb("mhalf", [P, 6])
    rb = off["kt"]

    def row(i):
        return WK[0:HEADS, rb + i * T:rb + (i + 1) * T]

    GI8 = WK[0:2 * HEADS, rb:rb + T]
    r9 = rb + 8 * T
    m0r = WK[0:HEADS, r9:r9 + NB + NPC + 1]
    wlr = WK[0:HEADS, r9 + 16:r9 + 29]
    wld = WK[0:HEADS, r9 + 32:r9 + 84].rearrange("p (h j) -> p h j", h=HEADS)
    assert r9 + 84 <= off["c0t"]

    out = [nc.alloc_psum_tensor(f"out{i}", [P, 2, 512], F32) for i in range(2)]
    BK = [nc.alloc_psum_tensor(f"bank{i}", [P, 512], F32) for i in (4, 5, 6, 7)]
    B4, B5, B6, B7 = BK

    def gout(n):
        return out[n % 2][:, :, 0:HALF]

    d_rows = nc.dram_tensor("d_rows", (HEADS, 2, T), F32, kind="Internal").ap()
    d_cache = nc.dram_tensor("d_cache", (P, KT, NB * PAD), F32, kind="Internal").ap()

    S = {}

    def sem(name):
        if name not in S:
            S[name] = nc.alloc_semaphore(name)
        return S[name]

    def wait(e, name, v):
        if isinstance(v, int) and v <= 0:
            return
        e.wait_ge(sem(name), v)

    class Chain:

        def __init__(self, e, name):
            self.e = e
            self.start(name)

        def start(self, name, per=0, i=0):
            self.name, self.per, self.i, self.v = name, per, i, 0

        def inc(self, ins):
            ins.then_inc(sem(self.name), 1)
            self.v = self.v + 1

        def wait(self):
            wait(self.e, self.name, self.per * self.i + self.v if self.per else self.v)

        def link(self, ins):
            self.inc(ins)
            self.wait()

    w_in = a["w_in"].rearrange("o (k p) n -> p (o k) n", p=P)
    w_m = a["w_branch_m"].rearrange("o (k p) n -> p (o k) n", p=P)
    w_c = a["w_branch_c"].rearrange("o (k p) n -> p (o k) n", p=P)
    w_o = a["w_out"].rearrange("o (k p) n -> p (o k) n", p=P)
    w_1 = a["w_ff1"].rearrange("o (k p) n -> p (o k) n", p=P)
    w_2 = a["w_ff2"].rearrange("o (k p) n -> p (o k) n", p=P)

    def pieces(t, lo=0):
        return [(t[:, 0, lo:HALF], slice(lo, HALF)), (t[:, 1, 0:HALF], slice(HALF, T))]


    def load_tile(sp, n, w, k0, col, more=0):
        need, at = val(n) - (NSTAGE - 1) + max(more, 0), col
        if n.per:
            need, k0, at = [x if isinstance(x, int) else sp.snap(x) for x in (need, k0, at)]
        src = w[:, k0:k0 + KT, bass.ds(at, P)] if isinstance(k0, int) else w[:, bass.ds(k0, KT), at:at + P]
        if not isinstance(need, int):
            sp.wait_ge(sem(f"ld{n.par}"), 16)
        if more >= 0:
            wait(sp, "w_lo", need)
        sp.dma_start(ST[:, n.par, :, :], src).then_inc(sem(f"ld{n.par}"), 16)

    def split_hi(act, n, par):
        act.wait_ge(sem(f"ld{par % NSTAGE}"), ldcount(n))
        wait(act, "tile_done", val(n) - 1)
        act.activation(WH[:, par % 2, :, :], ST[:, par % NSTAGE, :, :], ACT.Copy).then_inc(sem("w_hi"), 1)

    def split_lo(dve, n, par):
        wait(dve, "w_hi", val(n) + 1)
        dve.tensor_tensor(WL[:, par % 2, :, :], ST[:, par % NSTAGE, :, :],
                          WH[:, par % 2, :, :].bitcast(F32), ALU.subtract).then_inc(sem("w_lo"), 1)

    class N:

        def __init__(self, base, per=0, i=0):
            self.base, self.per, self.i = base, per, i

        def __add__(self, k):
            return N(self.base + k, self.per, self.i)

        @property
        def par(self):
            return self.base % 4

    def val(n):
        return n.base + n.per * n.i if n.per else n.base

    def ldcount(n):
        return 16 * (n.base // NSTAGE + 1) + (16 * n.per // NSTAGE) * n.i if n.per else 16 * (n.base // NSTAGE + 1)

    def ofcount(n):
        return n.base // 2 + (n.per // 2) * n.i if n.per else n.base // 2

    def evacuated(e, n):
        e.wait_ge(sem(f"of{n.par % 2}"), ofcount(n) + 1)

    def gemm(pe, n, xh, xl, gaps=(), rhs_ready=None):
        wait(pe, "w_lo", val(n) + 1)
        wait(pe, f"of{n.par % 2}", ofcount(n))
        s, ms = n.par % 2, []
        for kk in range(KT):
            for w, x in ((WH, xh), (WH, xl), (WL, xh)):
                for h in range(2):
                    ms.append((kk, w, x, h))
        cuts = [len(ms) * (g + 1) // (len(gaps) + 1) for g in range(len(gaps))]
        for m, (kk, w, x, h) in enumerate(ms):
            if m in cuts:
                gaps[cuts.index(m)]()
            if rhs_ready and m % 6 == 0:
                rhs_ready(kk)
            last = pe.matmul(out[s][:, h, 0:HALF], w[:, s, kk, :], x[:, kk, h * HALF:(h + 1) * HALF],
                             start=(m < 2), stop=(m >= len(ms) - 2))
        last.then_inc(sem("tile_done"), 1)

    def o_scaled(kk):
        return (tmp[4], tmp[5], tmp[1], tmp[3])[kk % 4]

    OUTC = [TS + NMETA + P * j for j in range(4)] + [0]

    with nc.Block() as block:
        @block.sync
        def _(sp):
            def dma(o, i, name, slow=False):
                return sp.dma_start(o, i, allow_slow_non_contiguous=slow).then_inc(sem(name), 16)

            def frames(to, name):
                for c in range(6):
                    src = (a["meta_tokens"] if c == 0 else a["x_sample"].rearrange("b t d -> (b t) d") if c == SMP
                           else a["x_prompt"][0, P * (c - 1):P * c, :])
                    dma(to[0:CHUNKS[c][1], c, :], src, f"{name}{c}")

            frames(xtok0, "xin")
            for i, nm in enumerate(VEC):
                dma(CVF[KT * i:KT * i + KT, 0:P], a[nm].rearrange("o (k p) -> (o k) p", p=P), "vecs")
            dma(bif[:, :], a["b_if"].rearrange("o h -> h o"), "smalls", True)
            dma(m0r[:, 0:NB], a["state_mlstm_m"].rearrange("o b h -> (o h) b"), "smalls", True)
            load_tile(sp, N(0), w_in, 0, OFF_I)
            dma(CVF[0:CONV_W, P:P + D], a["conv_w"][0], "vecs")
            dma(CVF[0:NB * HEADS, P + D:P + D + DH], a["state_mlstm_n"].rearrange("o b h d -> (o b h) d"), "vecs")
            cache = a["cache_conv"].rearrange("o (g b) w n -> g (o b w) n", g=2)
            for g in range(2):
                dma(CVF[0:4 * PAD, P + D + DH + g * D:P + D + DH + (g + 1) * D], cache[g, :, :], "cache")

            def head_loads(i):
                first = isinstance(i, int)
                n = N(N_HEADS0, PER_HEAD, i)
                cols = [o + x * P for o in (OFF_K, OFF_Q, OFF_V, OFF_O) for x in range(2)]
                cols += [o + x * P for x in range(2) for o in (OFF_CB, OFF_CA)]
                for r, col in enumerate(cols):
                    if r == 7 and first:
                        sp.wait_ge(sem("rows_out"), 32)
                        bc_load(d_rows[0:1, :, :])
                    elif r == 3 and not first:
                        gated = sp.snap(ofcount(n + -1) + 1)
                        tile, src = sp.snap((i - 1) * 2), d_rows[bass.ds(i, 1), :, :]
                        tile1 = sp.snap((i - 1) * 2 + 1)
                        sp.wait_ge(sem("rows_out"), 32)
                        sp.wait_ge(sem(f"of{(n + -1).par % 2}"), gated)
                        bc_load(src)
                        sp.wait_ge(sem("cache_out"), 16)
                        for x, tl in enumerate((tile, tile1)):
                            sp.dma_start(ups[:, x, :, 0:PAD], d_cache[:, bass.ds(tl, 1), :].rearrange(
                                "p o (b w) -> p (o b) w", b=NB)).then_inc(sem("cache_in"), 16)
                    load_tile(sp, n + r, w_in, 0, i * 2 * P + col)

            def bc_load(src):
                sp.dma_start(WK[:, off["bc"]:off["bc"] + 2 * T],
                             src.rearrange("h r t -> h (r t)").to_broadcast([P, 2 * T])).then_inc(sem("bc_in"), 16)

            sp.wait_ge(sem("cache_out"), 16)
            head_loads(0)
            with sp.Fori(1, HEADS) as i:
                head_loads(i)
            def gates_and_branch(i):
                for r, (w, o) in enumerate(((w_in, OFF_GM), (w_in, OFF_GM + P), (w_m, 0), (w_m, P))):
                    load_tile(sp, N(N_GM0, 4, i) + r, w, 0, i * 2 * P + o, 0 if isinstance(i, int) else {1: 1, 2: -1}.get(r, 0))

            gates_and_branch(0)
            sp.wait_ge(sem("conv"), 2 * TAPS * 3)
            for x in range(2):
                dma(ups[:, x, :, 0:PAD], d_cache[:, 6 + x, :].rearrange("p (b w) -> p b w", b=NB), "cache_in")
            with sp.Fori(1, KT // 2) as i:
                gates_and_branch(i)
            for n0, w, o in ((N_GC0, w_in, OFF_GC), (N_GC0 + KT, w_c, 0)):
                with sp.Fori(0, 2) as i:
                    for r in range(4):
                        load_tile(sp, N(n0, 4, i) + r, w, 0, i * 4 * P + (o + r * P))
            for r in range(4):
                load_tile(sp, N(N_OUT0 + r), w_o, 0, r * P)
            sp.wait_ge(sem("mg2"), KT)
            frames(xtok5, "xagain")
            for r in range(4, KT):
                load_tile(sp, N(N_OUT0 + r), w_o, 0, r * P)
            with sp.Fori(0, DFF // D) as c:
                n = N(N_FF0, 2 * KT, c)
                for r in range(KT):
                    load_tile(sp, n + r, w_1, 0, c * D + r * P)
                for r in range(KT):
                    load_tile(sp, n + (KT + r), w_2, c * KT, r * P)
            for c in range(5):
                wait(sp, "ytok", c + 1)
                o = a["o_y_sample"].rearrange("b t d -> (b t) d") if c == 4 else a["o_y_prompt"][0, P * c:P * c + P, :]
                dma(o, xtok5[:, c, :], "stores")
            sp.wait_ge(sem("stores"), 16 * 5)

        @block.gpsimd
        def _(g):
            g.memset(ident[:, :], 0.0).then_inc(sem("g_seq"), 1)
            g.memset(maskc[:, :], 0.0).then_inc(sem("g_seq"), 1)
            g.memset(maskd[:, :], 0.0).then_inc(sem("g_seq"), 1)
            g.memset(bmask[:, :], 1.0).then_inc(sem("g_seq"), 1)
            g.memset(mhalf[:, :], -0.5).then_inc(sem("mhalf"), 1)
            g.wait_ge(sem("g_seq"), 4)
            g.affine_select(out=ident[:, :], in_=ident[:, :], compare_op=ALU.not_equal, fill=1.0, base=0,
                            pattern=[[-1, P]], channel_multiplier=1).then_inc(sem("consts"), 1)
            g.affine_select(out=maskc[:, :], in_=maskc[:, :], compare_op=ALU.is_ge, fill=NEG, base=0,
                            pattern=[[1, P]], channel_multiplier=-1).then_inc(sem("consts"), 1)
            md = maskd[:, :].rearrange("p (b t) -> p b t", b=NB)
            g.affine_select(out=maskd[:, :], in_=maskd[:, :], compare_op=ALU.is_ge, fill=NEG, base=0,
                            pattern=[[1, P]], channel_multiplier=-1).then_inc(sem("g_seq"), 1)
            g.wait_ge(sem("g_seq"), 5)
            g.affine_select(out=md, in_=md, compare_op=ALU.is_ge, fill=NEG, base=0,
                            pattern=[[-LB, NB], [0, LB]], channel_multiplier=1).then_inc(sem("consts"), 1)
            g.affine_select(out=bmask[:, :], in_=bmask[:, :], compare_op=ALU.is_ge, fill=0.0, base=0,
                            pattern=[[-LB, NB]], channel_multiplier=1).then_inc(sem("g_seq"), 1)
            g.wait_ge(sem("g_seq"), 6)
            g.affine_select(out=bmask[:, :], in_=bmask[:, :], compare_op=ALU.is_ge, fill=0.0, base=LB - 1,
                            pattern=[[LB, NB]], channel_multiplier=-1).then_inc(sem("consts"), 1)
            g.wait_ge(sem("mhalf"), 1)
            g.wait_ge(sem("ovar"), 1)
            g.tensor_tensor(sm[:, 6:12], sm[:, 0:6], mhalf[:, :], ALU.pow).then_inc(sem("ort"), 1)
            g.wait_ge(sem("orr"), 2)
            for kk in range(1, KT, 2):
                wait(g, "x2", kk - 3)
                g.tensor_tensor(o_scaled(kk), CV[:, kk, :], tmp[2], ALU.mult).then_inc(sem("om1"), 1)
            for kk in range(KT):
                g.wait_ge(sem("x2"), kk + 1)
                g.memset(CV[:, kk, :], 0.0).then_inc(sem("y_zero"), 1)
            g.tensor_tensor(tmp[7], MG[:, 0, :], MG[:, 0, :], ALU.mult).then_inc(sem("fsum"), 1)
            for kk in range(1, KT):
                sq = (tmp[0], tmp[6])[kk % 2]
                g.tensor_tensor(sq, MG[:, kk, :], MG[:, kk, :], ALU.mult).then_inc(sem("fsum"), 1)
                g.wait_ge(sem("fsum"), 2 * kk)
                g.tensor_tensor(tmp[7], tmp[7], sq, ALU.add).then_inc(sem("fsum"), 1)
            g.wait_ge(sem("yvar"), 1)
            g.tensor_tensor(sm[:, 36:41], sm[:, 30:35], mhalf[:, 0:5], ALU.pow).then_inc(sem("yrt"), 1)

        @block.scalar
        def _(act):
            def copy(o, i, name, fn=ACT.Copy, **kw):
                act.activation(o, i, fn, **kw).then_inc(sem(name), 1)

            act.wait_ge(sem("v_consts"), 1)
            for c, (_, L) in enumerate(CHUNKS):
                act.wait_ge(sem(f"xin{c}"), 16)
                wait(act, "ss0", c)
                act.activation(out[0][0:L, :, :].rearrange("p h t -> p (h t)"), xtok0[0:L, c, :], ACT.Square,
                               accum_out=sm[0:L, c:c + 1]).then_inc(sem("ss0"), 1)
            act.wait_ge(sem("ms0"), 1)
            copy(sm[:, 12:18], sm[:, 6:12], "rt0", ACT.Sqrt)
            act.wait_ge(sem("t_par"), 1)
            copy(prm[:, :], B6[:, 0:64], "prm_ready")
            copy(n0t[:, :, :], B6[:, 64:128].rearrange("p (j b) -> p j b", j=2), "prm_ready")
            copy(cwt[:, :, :], B7[:, 0:KT * CONV_W].rearrange("p (k w) -> p k w", k=KT), "prm_ready")
            act.wait_ge(sem("prm_ready"), 3)
            for kk in range(KT):
                act.wait_ge(sem("t_cache"), kk + 1)
                copy(xc[:, kk, :], BK[kk % 2][:, 0:NB * PAD], "cache_sb")
            act.wait_ge(sem("cache_sb"), KT)
            act.dma_start(d_cache, xc).then_inc(sem("cache_out"), 16)
            for kk in range(KT):
                act.wait_ge(sem("t_x"), kk + 1)
                copy(XH[:, kk, TS + NMETA:T], out[kk % 2][:, 0, :], "xh", scale=vec("g_pre_mix", kk))
                copy(XH[:, kk, 0:TS + NMETA], out[kk % 2][:, 1, 0:TS + NMETA], "xh", scale=vec("g_pre_mix", kk))

            def hi(n):
                split_hi(act, n, n.par)

            def evac(n, o, fn=ACT.Copy, **kw):
                act.wait_ge(sem("tile_done"), val(n) + 1)
                act.activation(o, gout(n.par), fn, **kw).then_inc(sem(f"of{n.par % 2}"), 1)

            def two(ap):
                return ap.rearrange("p (h t) -> p h t", h=2)

            hi(N(0))
            hi(N(1))
            act.wait_ge(sem("smalls"), 32)
            act.wait_ge(sem("xl"), 2 * KT)
            act.wait_ge(sem("tile_done"), 1)
            act.activation(two(GI8), gout(0)[0:2 * HEADS], ACT.Identity, bias=bif[:, 0:1]).then_inc(sem("of0"), 1)
            act.wait_ge(sem("of0"), 1)
            act.dma_start(row(1), WK[HEADS:2 * HEADS, rb:rb + T]).then_inc(sem("f_rows"), 16)
            def rows_log():
                act.wait_ge(sem("r_nabs"), 1)
                copy(row(3), row(3), "r_e", ACT.Exp)
                act.wait_ge(sem("r_e"), 1)
                copy(row(4), row(3), "r_ln", ACT.Ln, bias=1.0)
                act.wait_ge(sem("r_ln"), 1)
                copy(row(5), row(4), "r_inv", ACT.Exp, scale=-1.0)

            def rows_exp():
                act.wait_ge(sem("r_args"), 1)
                copy(row(2), row(2), "r_exp", ACT.Exp)
                copy(row(4), row(4), "r_exp", ACT.Exp)
                copy(row(5), row(5), "r_exp", ACT.Exp)
                act.wait_ge(sem("r_exp"), 3)
                act.dma_start(d_rows[:, 0, :], row(6)).then_inc(sem("rows_out"), 16)
                act.dma_start(d_rows[:, 1, :], row(4)).then_inc(sem("rows_out"), 16)
                act.dma_start(a["o_m_prompt"].rearrange("o b h -> (o h) b"), row(7)[:, T - 1:T],
                              allow_slow_non_contiguous=True).then_inc(sem("m_out"), 16)
                act.dma_start(a["o_m_sample"].rearrange("o b h -> (o h) b"), row(7)[:, LB - 1:TS:LB],
                              allow_slow_non_contiguous=True).then_inc(sem("m_out"), 16)

            def rows_free():
                act.wait_ge(sem("cols"), 3)
                act.wait_ge(sem("rows_out"), 32)
                act.wait_ge(sem("m_out"), 32)

            def c0_load(i, b):
                wait(act, f"c1_out{b % C0RING}", 16 * ((NB // C0RING) * i + b // C0RING))
                act.dma_start(c0[:, b % C0RING, :, :],
                              a["state_mlstm_C"][0, b, bass.ds(i, 1), :, :].rearrange("o (i p) d -> p (o i) d", p=P)
                              ).then_inc(sem(f"c0_in{b % C0RING}"), 16)

            def c1_store(i, b):
                act.wait_ge(sem("c1"), NB * i + b + 1)
                act.dma_start(a["o_C_sample"][0, b, bass.ds(i, 1), :, :].rearrange("o (i p) d -> p (o i) d", p=P),
                              c0[:, b % C0RING, :, :]).then_inc(sem(f"c1_out{b % C0RING}"), 16)

            def u_rows(i):
                act.wait_ge(sem("t_u"), i + 1)
                copy(ust[0:UR, 0:512], B6[0:UR, :], "u_sb")
                copy(ust[0:UR, 512:1024], B7[0:UR, :], "u_sb")
                copy(ust[0:PAD, 1024:1280], B5[0:PAD, 0:256], "u_sb")
                act.wait_ge(sem("u_sb"), 3 * i + 3)
                for b in range(2):
                    act.dma_start(a["o_conv_sample"].rearrange("o (g b) w n -> b w (o g) n", b=2)[
                                      b, :, :, bass.ds(i * 2 * P, 2 * P)],
                                  ust[b * WIN:b * WIN + PAD, 0:1024].rearrange("p (g n) -> p g n", g=NB // 2)
                                  ).then_inc(sem("u_out"), 16)
                act.dma_start(a["o_conv_prompt"][0, 0, :, bass.ds(i * 2 * P, 2 * P)],
                              ust[0:PAD, 1024:1280]).then_inc(sem("u_out"), 16)

            def epilogue_root(i):
                act.wait_ge(sem("hvar"), i + 1)
                copy(sm[:, 30:36], sm[:, 24:30], "hrt", ACT.Sqrt)

            def epilogue_out(i):
                act.wait_ge(sem("t_ct"), i + 1)
                act.wait_ge(sem("t_int"), NB * i + NB)
                copy(wk(off["c0t"], 512), B7[:, :], "cp_sb")
                act.wait_ge(sem("cp_sb"), i + 1)
                act.dma_start(a["o_C_prompt"][0, 0, bass.ds(i, 1), :, :].rearrange("o (i p) d -> p (o i) d", p=P),
                              wk(off["c0t"], 512).rearrange("p (i d) -> p i d", i=2)).then_inc(sem("cp_out"), 16)
                act.dma_start(a["o_n_prompt"][0, 0, bass.ds(i, 1), :].rearrange("o (j p) -> p (o j)", p=P),
                              ct[:, :, 256], allow_slow_non_contiguous=True).then_inc(sem("np_out"), 16)
                act.wait_ge(sem("hmf"), i + 1)
                copy(GH[:, bass.ds(i * 2, 2), :], qw, "hm_hi")

            def tok(i, fill, bank, pair, dst):
                act.wait_ge(sem("t_kv"), 6 * i + fill)
                v = bank[:, 0:512].rearrange("p (c e) -> p c e", c=2)
                if pair == 0:
                    copy(dst[0:NMETA, 0, 0:DH], v[0:NMETA, 0, :], "kv_tok")
                    copy(dst[:, 1, 0:DH], v[:, 1, :], "kv_tok")
                else:
                    copy(dst[:, 2 * pair:2 * pair + 2, 0:DH], v, "kv_tok")

            def states_in(i):
                wait(act, "n1_out", 16 * i)
                act.dma_start(n0b[:, :], a["state_mlstm_n"][0, :, bass.ds(i, 1), :].rearrange("b o d -> b (o d)")
                              ).then_inc(sem("n0b_in"), 16)
                for b in range(C0RING):
                    c0_load(i, b)

            def exp_weights(i):
                act.wait_ge(sem("wt_arg"), i + 1)
                copy(bcm, bcm, "wt", ACT.Exp)

            def head(i):
                n = N(N_HEADS0, PER_HEAD, i)
                first = isinstance(i, int)
                hi(n + 1)
                if first:
                    rows_log()
                else:
                    epilogue_root(i - 1)
                evac(n, two(k[:, 0, :]), scale=DH ** -0.5)
                hi(n + 2)
                if not first:
                    epilogue_out(i - 1)
                    states_in(i)
                evac(n + 1, two(k[:, 1, :]), scale=DH ** -0.5)
                hi(n + 3)
                if not first:
                    exp_weights(i)
                    u_rows(i - 1)
                evac(n + 2, two(q[:, 0, :]))
                hi(n + 4)
                if first:
                    rows_exp()
                evac(n + 3, two(q[:, 1, :]))
                if not first:
                    tok(i, 1, B4, 0, ktok)
                    tok(i, 2, B5, 1, ktok)
                hi(n + 5)
                wait(act, "u_out", 48 * i)
                evac(n + 4, two(vf[:, 0, :]))
                if not first:
                    tok(i, 3, B4, 2, ktok)
                hi(n + 6)
                evac(n + 5, two(vf[:, 1, :]))
                if first:
                    rows_free()
                    states_in(i)
                    tok(i, 1, B4, 0, ktok)
                    tok(i, 2, B5, 1, ktok)
                hi(n + 7)
                if first:
                    exp_weights(i)
                evac(n + 6, two(so[:, 0, :]), ACT.Sigmoid)
                if first:
                    tok(i, 3, B4, 2, ktok)
                else:
                    tok(i, 4, B5, 0, vtok)
                    tok(i, 5, B4, 1, vtok)
                hi(n + 8)
                evac(n + 7, two(so[:, 1, :]), ACT.Sigmoid)
                if first:
                    tok(i, 4, B5, 0, vtok)
                    tok(i, 5, B4, 1, vtok)
                tok(i, 6, B6, 2, vtok)
                for s in range(NSLOT):
                    if s in (1, 4, 7, 10):
                        hi(n + (8 + (s - 1) // 3 + 1))
                    if s in TR_SLOT:
                        b = TR_SLOT[s]
                        act.wait_ge(sem("t_c0"), NB * i + b + 1)
                        wait(act, "t_int", NB * i + b)
                        if b == 0:
                            wait(act, "cp_out", 16 * i)
                        copy(wk(off["c0t"], 512), B4[:, :], "c0t_ready")
                    if s in NUM_SLOT and NUM_SLOT[s] < NPC:
                        numer(i, NUM_SLOT[s])
                    if s == 11:
                        act.wait_ge(sem("t_int"), NB * i + NB)
                        copy(wk(off["hti"], 256), B5[:, 128:384], "hti")
                    if s in STORE_SLOT:
                        c1_store(i, STORE_SLOT[s])
                    if s in LOAD_SLOT:
                        c0_load(i, LOAD_SLOT[s])
                    if s in (3, 9):
                        r = 8 if s == 3 else 10
                        if r == 8:
                            act.wait_ge(sem("qw_ready"), i + 1)
                        else:
                            evacuated(act, n + 9)
                        evac(n + r, two(bcw), ACT.Sigmoid)
                numer(i, SMP)
                act.wait_ge(sem("n1"), i + 1)
                act.dma_start(a["o_n_sample"][0, :, bass.ds(i, 1), :].rearrange("b o d -> b (o d)"), n0b[:, :]
                              ).then_inc(sem("n1_out"), 16)

            def numer(i, c):
                L = CHUNKS[c][1]
                act.wait_ge(sem("t_num"), 6 * i + c + 1)
                copy(num[0:L, c, :], B6[0:L, 0:257], "num")

            head(0)
            with act.Fori(1, HEADS) as i:
                head(i)

            def gates_m(i, early):
                n = N(N_GM0, 8, i)
                for g in range(2):
                    for r in range(2):
                        hi(n + (4 * g + r + 1))
                        if i or g:
                            evacuated(act, n + (4 * g - 2 + r))
                        evac(n + (4 * g + r), two(sg[:, r, :]), ACT.Sigmoid)
                        if g == 0:
                            early(r)
                    hi(n + (4 * g + 3))
                    hi(n + (4 * g + 4))

            def last_epilogue(r):
                if r == 0:
                    epilogue_root(HEADS - 1)
                else:
                    epilogue_out(HEADS - 1)
                    u_rows(HEADS - 1)

            gates_m(0, last_epilogue)
            gates_m(1, lambda r: None)
            for b in range(C0RING):
                act.wait_ge(sem(f"c1_out{b}"), 16 * HEADS * NB // C0RING)
            act.wait_ge(sem("cp_out"), 16 * HEADS)
            act.wait_ge(sem("u_out"), 16 * 3 * HEADS)
            for r in range(KT):
                hi(N(N_GC0 + r + 1))
                evac(N(N_GC0 + r), two(gcs[:, r, :]), ACT.Sigmoid)
                if r == 1:
                    act.wait_ge(sem("t_ln"), 1)
                    copy(ln[1][:, TS + NMETA:T], B4[:, :], "mean", scale=1.0 / D)
                    copy(ln[1][:, 0:TS + NMETA], B5[:, 0:TS + NMETA], "mean", scale=1.0 / D)
                if r == 2:
                    for kk in range(KT):
                        act.wait_ge(sem("cvc"), kk + 1)
                        wait(act, "lsq", kk - 1)
                        copy(ln[2 + kk % 2], CV[:, kk, :], "csq", ACT.Square)
                if r == 4:
                    act.wait_ge(sem("lvar"), 1)
                    copy(ln[1], ln[0], "lrt", ACT.Sqrt)
                if r == 6:
                    for kk in range(KT):
                        act.wait_ge(sem("cvn"), kk + 1)
                        copy(CV[:, kk, :], CV[:, kk, :], "cs", ACT.Silu, scale=vec("ln_g", kk), bias=vec("ln_b", kk))
            for kk in range(KT):
                act.wait_ge(sem("cs"), kk + 1)
                copy(GH[:, kk, :], CV[:, kk, :], "ch")
            for r in range(KT):
                hi(N(N_GC0 + KT + r + 1))
                act.wait_ge(sem("mg2"), r + 1)
                copy(XH[:, r, :], MG[:, r, :], "mh")
            for r in range(KT):
                n = N(N_OUT0 + r)
                hi(n + 1)
                act.wait_ge(sem("tile_done"), val(n) + 1)
                wait(act, "oacc", r - 1)
                act.activation(two(tmp[r % 2]), gout(n.par), ACT.Square).then_inc(sem("osq"), 1)
                evac(n, two(CV[:, r, :]), scale=vec("g_post_mix", r))
                act.wait_ge(sem("t_xa"), r + 1)
                act.wait_ge(sem("ml"), r + 1)
                b0, b1 = (B4, B5) if r % 2 == 0 else (B6, B7)
                copy(MG[:, r, TS + NMETA:T], b0[:, :], "xa")
                copy(MG[:, r, 0:TS + NMETA], b1[:, 0:TS + NMETA], "xa")
            act.wait_ge(sem("t_or"), 1)
            copy(tmp[2][:, TS + NMETA:T], B6[:, :], "orr")
            copy(tmp[2][:, 0:TS + NMETA], B7[:, 0:TS + NMETA], "orr")
            for kk in range(KT):
                act.wait_ge(sem("x2"), kk + 1)
                copy(XH[:, kk, :], MG[:, kk, :], "fh", scale=vec("g_pre_ffn", kk))

            def y_frames(r):
                act.wait_ge(sem("t_y"), r + 1)
                copy(CV[:, r, 0:4 * P], B4[:, :], "yt")
                copy(CV[:, r, 4 * P:5 * P], B5[:, 0:P], "yt")

            def ffn(c, last=False):
                n = N(N_FF0, 2 * KT, c)
                for r in range(KT):
                    hi(n + (r + 1))
                    evac(n + r, two(tmp[4 + r % 2]), ACT.Relu)
                    act.wait_ge(sem("hsq"), c * KT + (r + 1))
                    copy(GH[:, r, :], tmp[2 + r % 2], "hh")
                    if last:
                        act.wait_ge(sem("t_x2"), r + 1)
                        copy(xtok5[:, 0:4, r * P:r * P + P], B6[:, :].rearrange("p (c e) -> p c e", c=4), "x2t")
                        copy(xtok5[:, 4, r * P:r * P + P], B7[:, 0:P], "x2t")
                for r in range(KT):
                    if not last or r < KT - 1:
                        hi(n + (KT + 1 + r))
                    if last:
                        wait(act, "yacc", r - 1)
                        evacuated(act, n + (KT + r))
                        copy(tmp[r % 2], CV[:, r, :], "ysq", ACT.Square)
                        copy(CV[:, r, :], CV[:, r, :], "yg", scale=vec("g_post_ffn", r))
                        if r:
                            y_frames(r - 1)

            with act.Fori(0, DFF // D - 1) as c:
                ffn(c)
            ffn(DFF // D - 1, last=True)
            y_frames(KT - 1)
            act.wait_ge(sem("cache_out"), 16)
            act.wait_ge(sem("np_out"), 16 * HEADS)
            act.wait_ge(sem("n1_out"), 16 * HEADS)

        @block.vector
        def _(dve):
            V = Chain(dve, "v_seq")

            def two(ap):
                return ap.rearrange("p (h t) -> p h t", h=2)

            def lo(n):
                split_lo(dve, n, n.par)

            def tt(o, x, y, op):
                return dve.tensor_tensor(o, x, y, op)

            def stt(o, x, s, y, op0, op1):
                return dve.scalar_tensor_tensor(o, x, s, y, op0, op1)

            dve.memset(sm[:, :], 0.0)
            dve.memset(bst[:, :, :], 0.0)
            dve.memset(mv[:, :, :], 0.0)
            dve.memset(colA[:, :, :], 0.0)
            dve.memset(onesd[:, :], 1.0)
            V.link(dve.memset(up[:, :, 0:PAD], 0.0))
            dve.memset(ones[:, :], 1.0).then_inc(sem("v_consts"), 1)
            dve.wait_ge(sem("ss0"), 6)
            dve.tensor_scalar(sm[:, 6:12], sm[:, 0:6], 1.0 / D, EPS, ALU.mult, ALU.add).then_inc(sem("ms0"), 1)
            dve.wait_ge(sem("rt0"), 1)
            V.link(dve.reciprocal(sm[:, 18:24], sm[:, 12:18]))
            for c, (_, L) in enumerate(CHUNKS):
                dve.tensor_scalar(xtok0[0:L, c, :], xtok0[0:L, c, :], sm[0:L, 18 + c:19 + c], None,
                                  ALU.mult).then_inc(sem("xs"), 1)
            dve.wait_ge(sem("prm_ready"), 3)
            for kk in range(KT):
                for h, (p0, cols) in enumerate(((out[kk % 2][:, 0, :], slice(TS + NMETA, T)),
                                                (out[kk % 2][:, 1, 0:TS + NMETA], slice(0, TS + NMETA)))):
                    dve.wait_ge(sem("xh"), 2 * kk + h + 1)
                    stt(XL[:, kk, cols], p0, vec("g_pre_mix", kk), XH[:, kk, cols].bitcast(F32),
                        ALU.mult, ALU.subtract).then_inc(sem("xl"), 1)
            lo(N(0))
            lo(N(1))
            def rows_b():
                dve.wait_ge(sem("f_rows"), 16)
                V.link(dve.tensor_scalar(row(2), row(1), 0.0, None, ALU.min))
                stt(row(3), row(2), 2.0, row(1), ALU.mult, ALU.subtract).then_inc(sem("r_nabs"), 1)
                dve.wait_ge(sem("r_e"), 1)
                V.link(dve.tensor_scalar(row(6), row(3), 1.0, None, ALU.add))
                V.link(dve.tensor_scalar(row(6), row(6), -1.0, None, ALU.add))
                V.link(tt(row(6), row(3), row(6), ALU.subtract))
                dve.wait_ge(sem("r_inv"), 1)
                V.link(tt(row(6), row(6), row(5), ALU.mult))
                V.link(tt(row(6), row(6), row(4), ALU.add))
                V.link(tt(row(2), row(2), row(6), ALU.subtract))
                V.link(dve.memset(row(6), 1.0))
                V.link(dve.memset(row(6)[:, 0:TS:LB], 0.0))
                V.link(dve.memset(row(6)[:, TS:TS + 1], 0.0))
                V.link(dve.memset(row(6)[:, TS + NMETA:T:P], 0.0))
                V.link(dve.tensor_tensor_scan(row(1), row(6), row(2), 0.0, ALU.mult, ALU.add))
                V.link(tt(row(0), row(0), row(1), ALU.subtract))
                V.link(dve.memset(row(7), 0.0))
                V.link(dve.memset(m0r[:, NB:NB + 1], 0.0))
                dve.wait_ge(sem("smalls"), 32)

            def rows_max():
                for c, (c_, L) in enumerate(CHUNKS[:NPC]):
                    cs = slice(c_, c_ + L)
                    e_ = slice(c_ + L - 1, c_ + L)
                    m0 = m0r[:, NB + c:NB + c + 1]
                    V.link(dve.tensor_tensor_scan(row(3)[:, cs], row(7)[:, cs], row(0)[:, cs], m0, ALU.add, ALU.max))
                    V.link(tt(m0r[:, NB + c + 1:NB + c + 2], row(3)[:, e_], row(1)[:, e_], ALU.add))
                    V.link(dve.tensor_scalar(row(4)[:, cs], row(3)[:, cs], -1.0, m0, ALU.mult, ALU.add))
                    V.link(dve.tensor_scalar(row(2)[:, cs], row(0)[:, cs], row(3)[:, e_], None, ALU.subtract))
                for b in range(NB):
                    cs = slice(LB * b, LB * b + LB)
                    V.link(dve.tensor_tensor_scan(row(3)[:, cs], row(7)[:, cs], row(0)[:, cs], m0r[:, b:b + 1],
                                                  ALU.add, ALU.max))
                    V.link(dve.tensor_scalar(row(4)[:, cs], row(3)[:, cs], -1.0, m0r[:, b:b + 1], ALU.mult, ALU.add))
                    V.link(dve.tensor_scalar(row(2)[:, cs], row(0)[:, cs], row(3)[:, LB * b + LB - 1:LB * b + LB], None,
                                             ALU.subtract))
                V.link(tt(row(7), row(1), row(3), ALU.add))
                V.link(dve.tensor_scalar(row(5), row(7), -1.0, None, ALU.mult))
                dve.tensor_scalar(row(6), row(3), -1.0, None, ALU.mult).then_inc(sem("r_args"), 1)

            def rows_last():
                dve.wait_ge(sem("r_exp"), 3)
                V.link(dve.tensor_copy(wlr[:, 0:NPC], row(4)[:, TS + NMETA - 1:T:P]))
                V.link(dve.tensor_copy(wlr[:, NPC:13], row(4)[:, LB - 1:TS:LB]))
                dve.wait_ge(sem("consts"), 4)
                tt(wld[:, :, :], wlr[:, :].unsqueeze(1).to_broadcast([HEADS, HEADS, 13]),
                   ident[0:HEADS, 0:HEADS].unsqueeze(2).to_broadcast([HEADS, HEADS, 13]), ALU.mult).then_inc(sem("wld"), 1)

            def rows_columns():
                dve.wait_ge(sem("t_cols"), 1)
                dve.tensor_copy(colA[0:NMETA, :, 0:3], B4[0:NMETA, 0:12].rearrange("p (x h) -> p h x", h=HEADS)
                                ).then_inc(sem("cols"), 1)
                dve.tensor_copy(colA[:, :, 3:18], B4[:, 12:72].rearrange("p (x h) -> p h x", h=HEADS)
                                ).then_inc(sem("cols"), 1)
                V.inc(dve.tensor_copy(wlb[:, :], B5[0:NB, 64:64 + HEADS]))
                dve.tensor_copy(colA[:, :, 18:31], B5[:, 0:52].rearrange("p (h j) -> p h j", h=HEADS)
                                ).then_inc(sem("cols"), 1)
                dve.wait_ge(sem("cols"), 3)
                dve.wait_ge(sem("rows_out"), 32)
                dve.wait_ge(sem("m_out"), 32)
                V.link(dve.memset(vtok[:, :, DH:DH + 1], 1.0))

            def taps(u, y0, y1):
                for y in range(y0, min(y1, TAPS)):
                    x, t = divmod(y, CONV_W)
                    for part in range(2):
                        if part == 0:
                            src = up[:, x, t:t + TP]
                            dst = CV[:, bass.ds(u * 2 + x, 1), TS:T].rearrange("p o t -> p (o t)")
                        else:
                            src = ups[:, x, :, t:t + LB]
                            dst = CV[:, bass.ds(u * 2 + x, 1), 0:TS].rearrange("p o (b t) -> p (o b) t", b=NB)
                        if t == 0:
                            dve.tensor_scalar(dst, src, cwu[:, x, 0:1], cwu[:, x, CONV_W:CONV_W + 1],
                                              ALU.mult, ALU.add).then_inc(sem("conv"), 1)
                        else:
                            wait(dve, "conv", 2 * TAPS * u + (2 * y + part - 1))
                            stt(dst, src, cwu[:, x, t:t + 1], dst, ALU.mult, ALU.add).then_inc(sem("conv"), 1)
                return min(y1, TAPS)

            def unit_params(u):
                V.inc(dve.tensor_copy(cwu[:, :, 0:CONV_W], cwt[:, bass.ds(u * 2, 2), :]))
                V.inc(dve.tensor_copy(cwu[:, :, CONV_W], vec("conv_b", u * 2, 2)))
                V.link(dve.tensor_copy(ghd[:, :], vec("g_headnorm", u * 2, 2)))

            def epilogue_norm(i):
                den, mean, var = num[:, :, DH], mv[:, :, 0], mv[:, :, 1]
                emin = colH[:, 2:18:3]
                dve.wait_ge(sem("num"), 6 * i + 6)
                V.link(stt(sm[:, 18:24], den, -1.0, den, ALU.mult, ALU.max))
                V.inc(tt(sm[:, 18:24], sm[:, 18:24], emin, ALU.max))
                for c, (_, L) in enumerate(CHUNKS):
                    V.inc(dve.bn_aggr(mv[0:L, c, :], bst[0:L, c, :]))
                V.wait()
                V.link(dve.reciprocal(sm[:, 36:42], sm[:, 18:24]))
                V.link(tt(sm[:, 18:24], var, sm[:, 36:42], ALU.mult))
                V.link(tt(sm[:, 18:24], sm[:, 18:24], sm[:, 36:42], ALU.mult))
                dve.tensor_scalar(sm[:, 24:30], sm[:, 18:24], EPS, None, ALU.add).then_inc(sem("hvar"), 1)
                dve.wait_ge(sem("hrt"), i + 1)
                V.link(dve.reciprocal(sm[:, 18:24], sm[:, 30:36]))
                V.link(tt(sm[:, 36:42], sm[:, 36:42], sm[:, 18:24], ALU.mult))
                V.link(stt(sm[:, 42:48], mean, -1.0, sm[:, 36:42], ALU.mult, ALU.mult))
                for c, (_, L) in enumerate(CHUNKS):
                    dve.tensor_scalar(num[0:L, c, 0:DH], num[0:L, c, 0:DH], sm[0:L, 36 + c:37 + c],
                                      sm[0:L, 42 + c:43 + c], ALU.mult, ALU.add).then_inc(sem("hn"), 1)
                dve.wait_ge(sem("hn"), 6 * i + 6)

            def epilogue_gate(i):
                dve.wait_ge(sem("t_ht"), i + 1)
                for x in range(2):
                    stt(qw[:, x, TS + NMETA:T], (B4, B5)[x][:, :], ghd[:, x:x + 1], so[:, x, TS + NMETA:T],
                        ALU.mult, ALU.mult)
                for x in range(2):
                    ins = stt(qw[:, x, 0:TS + NMETA], B6[:, x * (TS + NMETA):(x + 1) * (TS + NMETA)],
                              ghd[:, x:x + 1], so[:, x, 0:TS + NMETA], ALU.mult, ALU.mult)
                ins.then_inc(sem("hmf"), 1)
                dve.wait_ge(sem("hm_hi"), i + 1)
                tt(GL[:, bass.ds(i * 2, 2), :], qw, GH[:, bass.ds(i * 2, 2), :].bitcast(F32),
                   ALU.subtract).then_inc(sem("hm_lo"), 1)

            def head_params(i):
                V.inc(dve.tensor_copy(colH[:, :], colA[:, bass.ds(i, 1), :].rearrange("p o x -> p (o x)")))
                V.link(dve.tensor_copy(nsel[:, :, :], n0v(i)))
                V.link(dve.tensor_scalar(wsb[:, :], bmask[:, :], colH[:, 3 * SMP + 1:3 * SMP + 2], None, ALU.mult))

            def n0v(i):
                return n0t[:, :, :].rearrange("p j (b h) -> p h j b", h=HEADS)[:, bass.ds(i, 1), :, :].rearrange(
                    "p o j b -> p (o j) b")

            def scores_weights(i):
                dve.wait_ge(sem("bc_in"), 16 * (i + 1))
                for c, (c_, L) in enumerate(CHUNKS):
                    mask = maskd if c == SMP else maskc
                    ins = stt(bcm[0:L, c_:c_ + L], bcm[0:L, c_:c_ + L], colH[0:L, 3 * c:3 * c + 1], mask[0:L, 0:L],
                              ALU.add, ALU.add)
                ins.then_inc(sem("wt_arg"), 1)

            def vws_next(i, u):
                kind, c = UPDATES[u]
                wait(dve, "t_upd", NUPD * i + u - 1)
                if kind == "U":
                    L = CHUNKS[c][1]
                    dve.tensor_scalar(vws[0:L, u % 2, :], vtok[0:L, c, :], colH[0:L, 3 * c + 1:3 * c + 2], None,
                                      ALU.mult).then_inc(sem("vws"), 1)
                else:
                    dve.tensor_scalar(vws[:, u % 2, :], vtok[:, SMP, :], wsb[:, c:c + 1], None,
                                      ALU.mult).then_inc(sem("vws"), 1)

            def update(i, u):
                kind, c = UPDATES[u]
                dve.wait_ge(sem("t_upd"), NUPD * i + u + 1)
                psum = B7[:, :].rearrange("p (j e) -> p j e", j=2)
                if kind == "D":
                    slot = c % C0RING
                    dve.wait_ge(sem(f"c0_in{slot}"), 16 * ((NB // C0RING) * i + c // C0RING + 1))
                    stt(c0[:, slot, :, :], c0[:, slot, :, :], colH[:, 23 + c:24 + c], psum, ALU.mult,
                        ALU.add).then_inc(sem("c1"), 1)
                elif c == 0:
                    wait(dve, "np_out", 16 * i)
                    dve.tensor_copy(ct[:, :, DH], B5[:, 384:386])
                    dve.tensor_copy(ct[:, :, 0:DH], psum).then_inc(sem("ct_ready"), 1)
                else:
                    dve.wait_ge(sem("ct_ready"), NPC * i + c)
                    stt(ct[:, :, DH], ct[:, :, DH], colH[:, 18 + c:19 + c], B5[:, 384:386], ALU.mult, ALU.add)
                    stt(ct[:, :, 0:DH], ct[:, :, 0:DH], colH[:, 18 + c:19 + c], psum, ALU.mult,
                        ALU.add).then_inc(sem("ct_ready"), 1)

            def stats(i, c):
                L = CHUNKS[c][1]
                dve.wait_ge(sem("num"), 6 * i + c + 1)
                V.inc(dve.bn_stats(bst[0:L, c, :], num[0:L, c, 0:DH]))

            def conv_input(i, r, x, n):
                dve.wait_ge(sem("tile_done"), val(n + r) + 1)
                evacuated(dve, n + (r - 1))
                wait(dve, "conv", 2 * TAPS * (i - 1) + (TAPS if x == 0 else 2 * TAPS))
                wait(dve, "t_u", i)
                p0 = gout((n + r).par)
                tt(ups[:, x, :, PAD:PAD + LB], p0[:, 0, 0:TS].rearrange("p (b t) -> p b t", b=NB),
                   bcw[:, 0:TS].rearrange("p (b t) -> p b t", b=NB), ALU.mult)
                tt(up[:, x, PAD:PAD + HALF - TS], p0[:, 0, TS:HALF], bcw[:, TS:HALF], ALU.mult)
                tt(up[:, x, PAD + HALF - TS:PL], p0[:, 1, :], bcw[:, HALF:T], ALU.mult
                   ).then_inc(sem(f"of{(n + r).par % 2}"), 1)

            def weigh_q(i):
                tt(qw, q, bcw.unsqueeze(1).to_broadcast([P, 2, T]), ALU.mult).then_inc(sem("qw_ready"), 1)
                dve.wait_ge(sem("qw_ready"), i + 1)

            def head(i):
                first = isinstance(i, int)
                n = N(N_HEADS0, PER_HEAD, i)
                lo(n + 1)
                if first:
                    rows_b()
                    lo(n + 2)
                    rows_max()
                    lo(n + 3)
                    lo(n + 4)
                    rows_last()
                    lo(n + 5)
                    rows_columns()
                    head_params(i)
                    lo(n + 6)
                    scores_weights(i)
                    evacuated(dve, n + 3)
                    weigh_q(i)
                    lo(n + 7)
                    lo(n + 8)
                else:
                    epilogue_norm(i - 1)
                    head_params(i)
                    lo(n + 2)
                    unit_params(i - 1)
                    epilogue_gate(i - 1)
                    scores_weights(i)
                    lo(n + 3)
                    dve.wait_ge(sem("cache_in"), 32 * i)
                    t = 0
                    for r in range(2, 8):
                        if r > 2:
                            lo(n + (r + 1))
                        if r == 3:
                            evacuated(dve, n + 3)
                            dve.wait_ge(sem("hm_lo"), i)
                            weigh_q(i)
                        t = taps(i - 1, t, t + CONV_TILE[r])
                dve.wait_ge(sem("kv_tok"), 8 * i + 8)
                vws_next(i, 0)
                vws_next(i, 1)
                u = 0
                for s in range(NSLOT):
                    if s in (1, 4, 7, 10):
                        lo(n + (8 + (s - 1) // 3 + 1))
                    if s in S_SLOT:
                        c = S_SLOT[s]
                        c_, L = CHUNKS[c]
                        dve.wait_ge(sem("t_s"), 6 * i + c + 1)
                        wait(dve, "t_num", 6 * i + c - 1)
                        if c == 0:
                            dve.wait_ge(sem("wt"), i + 1)
                        tt(pt[0:L, c % 2, 0:L], B5[0:L, 0:L], bcm[0:L, c_:c_ + L], ALU.mult).then_inc(sem("p_ready"), 1)
                    for kind in ("U", "D"):
                        if u < NUPD and UPDATES[u][0] == kind and (
                                (kind == "U" and NUM_SLOT.get(s) == UPDATES[u][1]) or
                                (kind == "D" and UPD_SLOT.get(s) == UPDATES[u][1])):
                            update(i, u)
                            if u + 2 < NUPD:
                                vws_next(i, u + 2)
                            u += 1
                    if s == 9:
                        tt(nqs.rearrange("p j (b t) -> p j b t", b=NB),
                           qw[:, :, 0:TS].rearrange("p j (b t) -> p j b t", b=NB),
                           nsel[:, :, :].unsqueeze(3).to_broadcast([P, 2, NB, LB]), ALU.mult).then_inc(sem("nq"), 1)
                    if s == 11:
                        dve.wait_ge(sem("t_n1"), i + 1)
                        dve.wait_ge(sem("n0b_in"), 16 * (i + 1))
                        wait(dve, "n1_out", 16 * i)
                        stt(n0b[:, :], n0b[:, :], wlb[:, bass.ds(i, 1)], B6[0:NB, 0:DH], ALU.mult,
                            ALU.add).then_inc(sem("n1"), 1)
                    if s in NUM_SLOT and NUM_SLOT[s] in (0, 1, 2, 3, 4):
                        stats(i, NUM_SLOT[s])
                    if not first and s in CONV_SLOT:
                        t = taps(i - 1, t, t + CONV_SLOT[s])
                    if s == 6:
                        conv_input(i, 9, 0, n)
                    if s == 12:
                        conv_input(i, 11, 1, n)
                stats(i, SMP)

            head(0)
            with dve.Fori(1, HEADS) as i:
                V.start("v_head", V_HEAD, i - 1)
                head(i)
                assert V.v == V_HEAD, V.v
            V.start("v_after")

            t = 0
            for j in range(2 * KT):
                n = N(N_GM0 + j)
                lo(n + 1)
                if j == 0:
                    epilogue_norm(HEADS - 1)
                if j == 1:
                    unit_params(HEADS - 1)
                    epilogue_gate(HEADS - 1)
                    dve.wait_ge(sem("cache_in"), 32 * HEADS)
                if j == 10:
                    dve.wait_ge(sem("u_out"), 48 * HEADS)
                if j % 4 >= 2:
                    kk = 2 * (j // 4) + j % 2
                    dve.wait_ge(sem("tile_done"), val(n) + 1)
                    evacuated(dve, n + -2)
                    tt(two(MG[:, kk, :]), gout(n.par), two(sg[:, j % 2, :]), ALU.mult
                       ).then_inc(sem(f"of{n.par % 2}"), 1)
                if j >= 1:
                    t = taps(HEADS - 1, t, t + 5)
            assert t == TAPS
            dve.wait_ge(sem("np_out"), 16 * HEADS)
            for r in range(KT):
                lo(N(N_GC0 + r + 1))
                if r == 0:
                    dve.wait_ge(sem("conv"), 2 * TAPS * HEADS)
                    V.link(tt(ln[0], CV[:, 0, :], CV[:, 1, :], ALU.add))
                    for kk in range(2, KT):
                        ins = tt(ln[0], ln[0], CV[:, kk, :], ALU.add)
                        if kk < KT - 1:
                            V.link(ins)
                    ins.then_inc(sem("lsum"), 1)
                if r == 2:
                    dve.wait_ge(sem("mean"), 2)
                    for kk in range(KT):
                        tt(CV[:, kk, :], CV[:, kk, :], ln[1], ALU.subtract).then_inc(sem("cvc"), 1)
                    for kk in range(KT):
                        dve.wait_ge(sem("csq"), kk + 1)
                        if kk == 0:
                            dve.tensor_copy(ln[4], ln[2]).then_inc(sem("lsq"), 1)
                        else:
                            dve.wait_ge(sem("lsq"), kk)
                            tt(ln[4], ln[4], ln[2 + kk % 2], ALU.add).then_inc(sem("lsq"), 1)
                if r == 4:
                    dve.wait_ge(sem("t_ln"), 2)
                    dve.tensor_scalar(ln[0][:, TS + NMETA:T], B4[:, :], 1.0 / D, EPS, ALU.mult, ALU.add)
                    dve.tensor_scalar(ln[0][:, 0:TS + NMETA], B5[:, 0:TS + NMETA], 1.0 / D, EPS, ALU.mult,
                                      ALU.add).then_inc(sem("lvar"), 1)
                if r == 5:
                    dve.wait_ge(sem("lrt"), 1)
                    V.link(dve.reciprocal(ln[0], ln[1]))
                    for kk in range(KT):
                        tt(CV[:, kk, :], CV[:, kk, :], ln[0], ALU.mult).then_inc(sem("cvn"), 1)
            for kk in range(KT):
                dve.wait_ge(sem("ch"), kk + 1)
                tt(GL[:, kk, :], CV[:, kk, :], GH[:, kk, :].bitcast(F32), ALU.subtract).then_inc(sem("cl"), 1)
            for r in range(KT):
                n = N(N_GC0 + KT + r)
                lo(n + 1)
                dve.wait_ge(sem("tile_done"), val(n) + 1)
                evacuated(dve, N(N_GC0 + r))
                tt(two(ln[r % 2]), gout(n.par), two(gcs[:, r, :]), ALU.mult).then_inc(sem(f"of{n.par % 2}"), 1)
                evacuated(dve, n)
                tt(MG[:, r, :], MG[:, r, :], ln[r % 2], ALU.add).then_inc(sem("mg2"), 1)
                dve.wait_ge(sem("mh"), r + 1)
                tt(XL[:, r, :], MG[:, r, :], XH[:, r, :].bitcast(F32), ALU.subtract).then_inc(sem("ml"), 1)

            def add_up(sq, name, acc, kk):
                dve.wait_ge(sem(sq), kk + 1)
                if kk == 0:
                    dve.tensor_copy(acc, tmp[0]).then_inc(sem(name), 1)
                else:
                    dve.wait_ge(sem(name), kk)
                    tt(acc, acc, tmp[kk % 2], ALU.add).then_inc(sem(name), 1)

            for r in range(KT):
                lo(N(N_OUT0 + r + 1))
                add_up("osq", "oacc", tmp[6], r)
            dve.wait_ge(sem("t_os"), 1)
            dve.tensor_scalar(sm[:, 0:6], B4[:, 0:6], 1.0 / D, EPS, ALU.mult, ALU.add).then_inc(sem("ovar"), 1)
            dve.wait_ge(sem("orr"), 2)
            for kk in range(0, KT + 3):
                if kk < KT and kk % 2 == 0:
                    tt(o_scaled(kk), CV[:, kk, :], tmp[2], ALU.mult).then_inc(sem("om0"), 1)
                if 0 < kk <= KT:
                    x = kk - 1
                    dve.wait_ge(sem("xa"), 2 * x + 2)
                    dve.wait_ge(sem(f"om{x % 2}"), x // 2 + 1)
                    tt(MG[:, x, :], o_scaled(x), MG[:, x, :], ALU.add).then_inc(sem("x2"), 1)
                if kk > 2:
                    x = kk - 3
                    dve.wait_ge(sem("fh"), x + 1)
                    stt(XL[:, x, :], MG[:, x, :], vec("g_pre_ffn", x), XH[:, x, :].bitcast(F32),
                        ALU.mult, ALU.subtract).then_inc(sem("fl"), 1)

            def ffn_factors():
                dve.wait_ge(sem("t_fs"), 1)
                V.link(dve.tensor_scalar(sm[:, 12:17], B5[:, 0:5], 1.0 / D, EPS, ALU.mult, ALU.add))
                V.link(dve.reciprocal(sm[:, 18:23], sm[:, 12:17]))
                V.link(stt(sm[:, 24:29], sm[:, 18:23], 1.0 / D, sm[:, 18:23], ALU.mult, ALU.mult))

            def ffn(c, last=False):
                n = N(N_FF0, 2 * KT, c)
                for r in range(KT):
                    lo(n + (r + 1))
                    evacuated(dve, n + r)
                    tt(tmp[2 + r % 2], tmp[4 + r % 2], tmp[4 + r % 2], ALU.mult).then_inc(sem("hsq"), 1)
                    dve.wait_ge(sem("hh"), c * KT + (r + 1))
                    tt(GL[:, r, :], tmp[2 + r % 2], GH[:, r, :].bitcast(F32), ALU.subtract).then_inc(sem("hl"), 1)
                for r in range(KT):
                    if not last or r < KT - 1:
                        lo(n + (KT + 1 + r))
                    if last and r > 0:
                        add_up("ysq", "yacc", tmp[6], r - 1)
                    dve.wait_ge(sem("tile_done"), val(n + (KT + r)) + 1)
                    dve.wait_ge(sem("y_zero"), r + 1)
                    tt(two(CV[:, r, :]), gout((n + (KT + r)).par), two(CV[:, r, :]), ALU.add
                       ).then_inc(sem(f"of{(n + r).par % 2}"), 1)

            with dve.Fori(0, DFF // D - 1) as c:
                ffn(c)
            ffn_factors()
            ffn(DFF // D - 1, last=True)
            add_up("ysq", "yacc", tmp[6], KT - 1)
            dve.wait_ge(sem("t_ys"), 1)
            V.link(tt(sm[:, 30:35], B7[:, 0:5], sm[:, 24:29], ALU.mult))
            dve.tensor_scalar(sm[:, 30:35], sm[:, 30:35], EPS, None, ALU.add).then_inc(sem("yvar"), 1)
            dve.wait_ge(sem("yrt"), 1)
            V.link(tt(sm[:, 42:47], sm[:, 36:41], sm[:, 18:23], ALU.mult))
            dve.wait_ge(sem("yt"), 2 * KT)
            for j in range(5):
                to = xtok5[:, j, :].rearrange("p (k e) -> p k e", k=KT)
                stt(to, CV[:, :, j * P:j * P + P], sm[:, 42 + j:43 + j], to, ALU.mult, ALU.add
                    ).then_inc(sem("ytok"), 1)

        @block.tensor
        def _(pe):
            def tr(o, i, name=None):
                r = i.shape[0]
                ins = pe.transpose(o, i, ident[0:r, 0:r])
                if name:
                    ins.then_inc(sem(name), 1)

            def mm(o, l, r, start=True, stop=True):
                return pe.matmul(o, l, r, start=start, stop=stop)

            pe.wait_ge(sem("consts"), 4)
            pe.wait_ge(sem("v_consts"), 1)
            pe.wait_ge(sem("vecs"), 16 * (len(VEC) + 2))
            tr(B6[:, 0:64], CVF[0:64, 0:P])
            for j in range(2):
                tr(B6[:, 64 + 32 * j:96 + 32 * j], CVF[0:32, P + D + P * j:P + D + P * j + P])
            for kk in range(KT):
                tr(B7[:, CONV_W * kk:CONV_W * kk + CONV_W], CVF[0:CONV_W, P + P * kk:2 * P + P * kk],
                   "t_par" if kk == KT - 1 else None)
            pe.wait_ge(sem("cache"), 32)
            for kk in range(KT):
                wait(pe, "cache_sb", kk - 1)
                for g in range(2):
                    o = P + D + DH + g * D + kk * P
                    tr(BK[kk % 2][:, g * 4 * PAD:(g + 1) * 4 * PAD], CVF[0:4 * PAD, o:o + P],
                       "t_cache" if g else None)
            pe.wait_ge(sem("xs"), 6)
            for kk in range(KT):
                wait(pe, "xl", 2 * (kk - 1))
                for c in range(1, 5):
                    tr(out[kk % 2][:, 0, P * (c - 1):P * c], xtok0[:, c, kk * P:kk * P + P])
                tr(out[kk % 2][:, 1, 0:TS], xtok0[:, SMP, kk * P:kk * P + P])
                tr(out[kk % 2][:, 1, TS:TS + NMETA], xtok0[0:NMETA, 0, kk * P:kk * P + P], "t_x")
            pe.wait_ge(sem("xl"), 2 * KT)
            gemm(pe, N(0), XH, XL)
            def columns():
                pe.wait_ge(sem("wld"), 1)
                for c, (c_, L) in enumerate(CHUNKS):
                    for x, rr in enumerate((0, 2, 5)):
                        o = (3 * c + x) * HEADS
                        tr(B4[0:L, o:o + HEADS], row(rr)[:, c_:c_ + L])
                mm(B5[:, 0:52], ones[0:HEADS, :], wld[:, :, :].rearrange("p h j -> p (h j)"))
                tr(B5[0:NB, 64:64 + HEADS], wlr[:, NPC:13], "t_cols")

            def headnorm_out(i):
                pe.wait_ge(sem("hn"), 6 * i + 6)
                pe.wait_ge(sem("c0t_ready"), NB * i + NB)
                pe.wait_ge(sem("hti"), i + 1)
                for x in range(2):
                    for c in range(1, 5):
                        tr((B4, B5)[x][:, P * (c - 1):P * c], num[:, c, x * P:x * P + P])
                for x in range(2):
                    o = x * (TS + NMETA)
                    tr(B6[:, o:o + TS], num[:, SMP, x * P:x * P + P])
                    tr(B6[:, o + TS:o + TS + NMETA], num[0:NMETA, 0, x * P:x * P + P], "t_ht" if x else None)
                pe.wait_ge(sem("c1"), NB * i + NB)
                pe.wait_ge(sem("ct_ready"), NPC * i + NPC)
                for e in range(2):
                    for j in range(2):
                        tr(B7[:, e * DH + j * P:e * DH + j * P + P], ct[:, j, e * P:e * P + P],
                           "t_ct" if e and j else None)

            def u_out(i, n):
                evacuated(pe, n + 9)
                evacuated(pe, n + 11)
                pe.wait_ge(sem("hmf"), i + 1)
                pe.wait_ge(sem("cp_sb"), i + 1)
                pe.wait_ge(sem("cache_in"), 32 * (i + 1))
                for g in range(NB // 2):
                    o = PL + 2 * g * WIN + LB
                    for x in range(2):
                        tr((B6, B7)[g // 2][0:UR, (g % 2) * 256 + x * P:(g % 2) * 256 + x * P + P], up[:, x, o:o + UR])
                for x in range(2):
                    tr(B5[0:PAD, x * P:x * P + P], up[:, x, TP:PL], "t_u" if x else None)

            def by_frame(src, bank, pair):
                for c in range(2 * pair, 2 * pair + 2):
                    c_, L = CHUNKS[c]
                    for x in range(2):
                        o = (c % 2) * DH + x * P
                        tr(bank[0:L, o:o + P], src[:, x, c_:c_ + L], "t_kv" if c % 2 and x else None)

            def slot(i, s):
                if s in NUM_SLOT:
                    pe.wait_ge(sem("p_ready"), 6 * i + NUM_SLOT[s] + 1)
                    wait(pe, "num", 6 * i + NUM_SLOT[s])
                if s in TR_SLOT:
                    b = TR_SLOT[s]
                    if b == 0:
                        pe.wait_ge(sem("kv_tok"), 8 * i + 8)
                    wait(pe, "c0t_ready", NB * i + b)
                    pe.wait_ge(sem(f"c0_in{b % C0RING}"), 16 * ((NB // C0RING) * i + b // C0RING + 1))
                    for e in range(2):
                        for j in range(2):
                            tr(B4[:, j * DH + e * P:j * DH + e * P + P], c0[:, b % C0RING, e, j * P:j * P + P],
                               "t_c0" if e and j else None)
                if s in S_SLOT or s in INT_SLOT or NUM_SLOT.get(s, NPC) < NPC:
                    wait(pe, "p_ready", 6 * i + sum(x < s for x in S_SLOT))
                    wait(pe, "ct_ready", NPC * i + sum(x < s and c < NPC for x, c in NUM_SLOT.items()))
                if s in INT_SLOT:
                    b = INT_SLOT[s]
                    pe.wait_ge(sem("c0t_ready"), NB * i + b + 1)
                    if b == 0:
                        pe.wait_ge(sem("qw_ready"), i + 1)
                    for e in range(2):
                        for j in range(2):
                            o = P + e * P + b * LB
                            ins = mm(B5[:, o:o + LB], c0t[:, j, e * P:e * P + P], qw[:, j, b * LB:b * LB + LB],
                                     j == 0, j == 1)
                    ins.then_inc(sem("t_int"), 1)
                if s in S_SLOT:
                    c = S_SLOT[s]
                    c_, L = CHUNKS[c]
                    if c == 0:
                        pe.wait_ge(sem("kv_tok"), 8 * i + 8)
                    for x in range(2):
                        ins = mm(B5[0:L, 0:L], k[:, x, c_:c_ + L], q[:, x, c_:c_ + L], x == 0, x == 1)
                    ins.then_inc(sem("t_s"), 1)
                if s == 11:
                    pe.wait_ge(sem("num"), 6 * i + NPC)
                    mm(B6[0:NB, 0:DH], wsb[:, :], ktok[:, SMP, :]).then_inc(sem("t_n1"), 1)
                if s in NUM_SLOT:
                    c = NUM_SLOT[s]
                    c_, L = CHUNKS[c]
                    o = B6[0:L, 0:257]
                    if c == 0:
                        ins = mm(o, pt[0:L, 0, 0:L], vtok[0:L, c, :])
                    elif c < NPC:
                        pe.wait_ge(sem("ct_ready"), NPC * i + c)
                        mm(o, pt[0:L, c % 2, 0:L], vtok[0:L, c, :], True, False)
                        for j in range(2):
                            ins = mm(o, qw[:, j, c_:c_ + L], ct[:, j, :], False, j == 1)
                    else:
                        pe.wait_ge(sem("n1"), i + 1)
                        pe.wait_ge(sem("hti"), i + 1)
                        pe.wait_ge(sem("nq"), i + 1)
                        mm(o, pt[:, c % 2, :], vtok[:, c, :], True, False)
                        for e in range(2):
                            mm(B6[:, e * P:e * P + P], hti[:, e, :], ident[:, :], False, False)
                        for j in range(2):
                            ins = mm(B6[:, DH:DH + 1], nqs[:, j, :], onesd[:, :], False, j == 1)
                    ins.then_inc(sem("t_num"), 1)
                for u, (kind, c) in enumerate(UPDATES):
                    if (NUM_SLOT if kind == "U" else UPD_SLOT).get(s) != c:
                        continue
                    pe.wait_ge(sem("vws"), NUPD * i + u + 1)
                    if u:
                        if UPDATES[u - 1][0] == "U":
                            pe.wait_ge(sem("ct_ready"), NPC * i + UPDATES[u - 1][1] + 1)
                        else:
                            pe.wait_ge(sem("c1"), NB * i + UPDATES[u - 1][1] + 1)
                    else:
                        wait(pe, "cp_sb", i)
                    w = vws[:, u % 2, :]
                    if kind == "U":
                        L = CHUNKS[c][1]
                        for j in range(2):
                            mm(B5[:, 384 + j:385 + j], ktok[0:L, c, j * P:j * P + P], w[0:L, DH:DH + 1])
                        for j in range(2):
                            ins = mm(B7[:, j * DH:j * DH + DH], ktok[0:L, c, j * P:j * P + P], w[0:L, 0:DH])
                    else:
                        for e in range(2):
                            ins = mm(B7[:, e * DH:e * DH + DH], w[:, e * P:e * P + P], ktok[:, SMP, :])
                    ins.then_inc(sem("t_upd"), 1)

            def head(i):
                first = isinstance(i, int)
                n = N(N_HEADS0, PER_HEAD, i)
                for r in range(PER_HEAD):
                    if r < 8:
                        gemm(pe, n + r, XH, XL)
                    else:
                        gemm(pe, n + r, XH, XL, gaps=[lambda s=3 * (r - 8) + g: slot(i, s) for g in (1, 2)])
                        slot(i, 3 * (r - 8) + 3)
                    if r == 0 and not first:
                        headnorm_out(i - 1)
                    if r == 1 and not first:
                        u_out(i - 1, n + -PER_HEAD)
                    if r == 4 and first:
                        columns()
                    if r == (5 if first else 3):
                        evacuated(pe, n + 1)
                        if first:
                            pe.wait_ge(sem("cols"), 3)
                        else:
                            pe.wait_ge(sem("hmf"), i)
                            pe.wait_ge(sem("u_sb"), 3 * i)
                        by_frame(k, B4, 0)
                        by_frame(k, B5, 1)
                    if r == (6 if first else 4):
                        pe.wait_ge(sem("kv_tok"), 8 * i + 2)
                        by_frame(k, B4, 2)
                    if r == (7 if first else 6):
                        evacuated(pe, n + 5)
                        pe.wait_ge(sem("kv_tok"), 8 * i + 4)
                        by_frame(vf, B5, 0)
                        by_frame(vf, B4, 1)
                    if r == 7:
                        by_frame(vf, B6, 2)
                        slot(i, 0)
                slot(i, 13)

            head(0)
            with pe.Fori(1, HEADS) as i:
                head(i)
            for j in range(2 * KT):
                if j % 4 < 2:
                    gemm(pe, N(N_GM0 + j), XH, XL)
                else:
                    gemm(pe, N(N_GM0 + j), GH, GL, rhs_ready=(lambda kk: kk == 6 and pe.wait_ge(sem("hm_lo"), HEADS))
                         if j == 2 else None)
                if j == 0:
                    headnorm_out(HEADS - 1)
                if j == 1:
                    u_out(HEADS - 1, N(N_HEADS0 + PER_HEAD * (HEADS - 1)))

            def channel_sum(acc, b0, b1, name):
                mm(b0[:, :], ones[:, :], acc[:, TS + NMETA:T])
                mm(b1[:, 0:TS + NMETA], ones[:, :], acc[:, 0:TS + NMETA]).then_inc(sem(name), 1)

            def frame_sums(acc, bank, starts, name):
                for j, c_ in enumerate(starts):
                    ins = mm(bank[:, j:j + 1], acc[:, c_:c_ + P], onesd[:, :])
                ins.then_inc(sem(name), 1)

            for r in range(KT):
                gemm(pe, N(N_GC0 + r), XH, XL)
                if r == 1:
                    pe.wait_ge(sem("lsum"), 1)
                    channel_sum(ln[0], B4, B5, "t_ln")
                if r == 3:
                    pe.wait_ge(sem("lsq"), KT)
                    pe.wait_ge(sem("mean"), 2)
                    channel_sum(ln[4], B4, B5, "t_ln")
            for r in range(KT):
                gemm(pe, N(N_GC0 + KT + r), GH, GL,
                     rhs_ready=(lambda kk: pe.wait_ge(sem("cl"), kk + 1)) if r == 0 else None)
            for r in range(KT):
                gemm(pe, N(N_OUT0 + r), XH, XL,
                     rhs_ready=(lambda kk: pe.wait_ge(sem("ml"), kk + 1)) if r == 0 else None)
                if r == 0:
                    for c in range(6):
                        pe.wait_ge(sem(f"xagain{c}"), 16)
                b0, b1 = (B4, B5) if r % 2 == 0 else (B6, B7)
                wait(pe, "xa", 2 * (r - 1))
                for c in range(1, 5):
                    tr(b0[:, P * (c - 1):P * c], xtok5[:, c, r * P:r * P + P])
                tr(b1[:, 0:TS], xtok5[:, SMP, r * P:r * P + P])
                tr(b1[:, TS:TS + NMETA], xtok5[0:NMETA, 0, r * P:r * P + P], "t_xa")
            pe.wait_ge(sem("oacc"), KT)
            pe.wait_ge(sem("xa"), 2 * KT)
            frame_sums(tmp[6], B4, [c_ if c else TS for c, (c_, _) in enumerate(CHUNKS)], "t_os")
            pe.wait_ge(sem("ort"), 1)
            for c in range(1, 5):
                mm(B6[:, P * (c - 1):P * c], sm[:, 6 + c:7 + c].to_broadcast([P, P]), ident[:, :])
            mm(B7[:, 0:TS], sm[:, 6 + SMP:7 + SMP].to_broadcast([P, P]), ident[:, :])
            mm(B7[:, TS:TS + NMETA], sm[:, 6:7].to_broadcast([P, P]), ident[:, 0:NMETA]).then_inc(sem("t_or"), 1)

            def by_frames(src, b0, b1, name):
                for j, c_ in enumerate(OUTC):
                    tr(b0[:, P * j:P * j + P] if j < 4 else b1[:, 0:P], src[:, c_:c_ + P], name if j == 4 else None)

            def ffn(c, last=False):
                n = N(N_FF0, 2 * KT, c)
                if last:
                    pe.wait_ge(sem("fsum"), 2 * KT - 1)
                    frame_sums(tmp[7], B5, OUTC, "t_fs")
                for r in range(KT):
                    gemm(pe, n + r, XH, XL, rhs_ready=(lambda kk: pe.wait_ge(sem("fl"), kk + 1)) if r == 0 else None)
                    if last:
                        wait(pe, "x2t", 2 * r)
                        by_frames(MG[:, r, :], B6, B7, "t_x2")
                for r in range(KT):
                    gemm(pe, n + (KT + r), GH, GL,
                         rhs_ready=(lambda kk: pe.wait_ge(sem("hl"), c * KT + (kk + 1))) if r == 0 else None)
                    if last and r:
                        y_frames(r - 1)

            def y_frames(r):
                pe.wait_ge(sem("yg"), r + 1)
                wait(pe, "yt", 2 * r)
                by_frames(CV[:, r, :], B4, B5, "t_y")

            with pe.Fori(0, DFF // D - 1) as c:
                ffn(c)
            ffn(DFF // D - 1, last=True)
            pe.wait_ge(sem("yacc"), KT)
            pe.wait_ge(sem("x2t"), 2 * KT)
            frame_sums(tmp[6], B7, OUTC, "t_ys")
            y_frames(KT - 1)


_INS = ["x_prompt", "x_sample", "state_mlstm_C", "state_mlstm_n", "state_mlstm_m", "cache_conv", "meta_tokens",
        "g_pre_mix", "w_in", "b_if", "g_headnorm", "w_branch_m", "conv_w", "conv_b", "ln_g", "ln_b", "w_branch_c",
        "w_out", "g_post_mix", "g_pre_ffn", "w_ff1", "w_ff2", "g_post_ffn"]
_OUTS = [("o_y_prompt", (1, SEQ, D)), ("o_y_sample", (NB, LB, D)), ("o_C_prompt", (1, 1, HEADS, DH, DH)),
         ("o_n_prompt", (1, 1, HEADS, DH)), ("o_m_prompt", (1, 1, HEADS)), ("o_conv_prompt", (1, 1, PAD, D)),
         ("o_C_sample", (1, NB, HEADS, DH, DH)), ("o_n_sample", (1, NB, HEADS, DH)), ("o_m_sample", (1, NB, HEADS)),
         ("o_conv_sample", (1, NB, PAD, D))]


def kernel(**inputs):
    import concourse.bacc as bacc
    from concourse.bass_utils import run_bass_kernel_spmd

    nc = bacc.Bacc("TRN2", target_bir_lowering=False, num_devices=1)
    arrays, aps = {}, {}
    for name in _INS:
        x = np.ascontiguousarray(inputs[name])
        arrays["in_" + name] = x
        aps[name] = nc.dram_tensor("in_" + name, x.shape, mybir.dt.from_np(x.dtype), kind="ExternalInput").ap()
    for name, shape in _OUTS:
        aps[name] = nc.dram_tensor(name, shape, F32, kind="ExternalOutput").ap()
    build(nc, aps)
    r = run_bass_kernel_spmd(nc, [arrays], core_ids=[0])
    return tuple(r.results[0][name] for name, _ in _OUTS)
```

```python
import numpy as np
import concourse.bass as bass
from concourse import mybir

F32 = mybir.dt.float32
R32 = mybir.dt.float32r
ALU = mybir.AluOpType
ACT = mybir.ActivationFunctionType

D = 1024
P = 128
KT = D // P
HEADS, DH = 4, 256
CONV_W = 31
PAD = CONV_W - 1
DFF = 4 * D
NMETA, SEQ = 16, 512
NB, LB = 8, 16
EPS = 1e-6
OFF_Q, OFF_K, OFF_V, OFF_O = 0, D, 2 * D, 3 * D
OFF_I = 4 * D
OFF_CA = OFF_I + 2 * HEADS
OFF_CB, OFF_GM, OFF_GC = OFF_CA + D, OFF_CA + 2 * D, OFF_CA + 3 * D
N_IN = OFF_GC + D

TS = NB * LB
TP = NMETA + SEQ
T = TS + TP
HALF = T // 2
P0 = NMETA + TS
T2 = T - NMETA
HALF2 = T2 // 2
NEG = -1e30
CHUNKS = [(0, NMETA)] + [(P0 + P * c, P) for c in range(SEQ // P)] + [(NMETA, TS)]
NPC = 5
SMP = 5

PER_HEAD = 12
N_HEADS0 = 1
N_GM0 = N_HEADS0 + PER_HEAD * HEADS
N_GC0 = N_GM0 + 2 * KT
N_OUT0 = N_GC0 + 2 * KT
N_FF0 = N_OUT0 + KT
NSTAGE = 4

S_SLOT = {0: 0, 2: 1, 4: 2, 6: 3, 8: 4, 10: 5}
NUM_SLOT = {1: 0, 3: 1, 5: 2, 7: 3, 9: 4, 13: 5}
UPD_SLOT = {0: 0, 2: 1, 4: 2, 6: 3, 8: 4, 10: 5, 11: 6, 12: 7}
TR_SLOT = {0: 0, 1: 1, 2: 2, 3: 3, 5: 4, 6: 5, 8: 6, 10: 7}
INT_SLOT = {1: 0, 2: 1, 3: 2, 4: 3, 6: 4, 7: 5, 9: 6, 11: 7}
NSLOT = 14
UPDATES = []
for _s in range(NSLOT):
    if _s in NUM_SLOT and NUM_SLOT[_s] < NPC:
        UPDATES.append(("U", NUM_SLOT[_s]))
    if _s in UPD_SLOT:
        UPDATES.append(("D", UPD_SLOT[_s]))
V_HEAD = 26
NUPD = len(UPDATES)
C0RING = 4
STORE_SLOT = {_s + 1: _b for _s, _b in UPD_SLOT.items()}
LOAD_SLOT = {_s + 2: _b + C0RING for _s, _b in UPD_SLOT.items() if _b + C0RING < NB}
CONV_TILE = {2: 7, 3: 4, 4: 7, 5: 7, 6: 7, 7: 3}
CONV_SLOT = {s: 2 if s % 2 else 3 for s in range(NSLOT) if 0 < s < 12}
TAPS = 2 * CONV_W
assert sum(CONV_TILE.values()) + sum(CONV_SLOT.values()) >= TAPS


def build(nc, a):
    def sb(name, shape, dt=F32):
        return nc.alloc_sbuf_tensor(name, shape, dt)

    XH, XL = sb("XH", [P, KT, T], R32), sb("XL", [P, KT, T], R32)
    XH2, XL2 = XH[:, :, NMETA:T], XL[:, :, NMETA:T]
    GH, GL = sb("GH", [P, KT, T2], R32), sb("GL", [P, KT, T2], R32)
    CV = sb("CV", [P, KT, T2])
    ST = sb("ST", [P, NSTAGE, KT, P])
    WH, WL = sb("WH", [P, 2, KT, P], R32), sb("WL", [P, 2, KT, P], R32)
    sizes = [("q", 2 * T), ("k", 2 * T), ("qw", 2 * T), ("vn", 6 * 257), ("so", 2 * T), ("kt", 6 * 256),
             ("vt", 6 * 257), ("vws", 2 * 257), ("c0", C0RING * 512), ("c0t", 512), ("hti", 256),
             ("pt", 2 * P), ("bc", 2 * T), ("ct", 2 * 257), ("up", 2 * (PAD + TP + NB * (PAD + LB)))]
    off, total = {}, 0
    for nm, n in sizes:
        off[nm] = total
        total += n
    WK = sb("WK", [P, total])

    def wk(o, n):
        return WK[:, o:o + n]

    q = wk(off["q"], 2 * T).rearrange("p (a t) -> p a t", a=2)
    k = wk(off["k"], 2 * T).rearrange("p (a t) -> p a t", a=2)
    qw = wk(off["qw"], 2 * T).rearrange("p (a t) -> p a t", a=2)
    vf = wk(off["vn"], 2 * T).rearrange("p (a t) -> p a t", a=2)
    num = wk(off["vn"], 6 * 257).rearrange("p (c e) -> p c e", c=6)
    so = wk(off["so"], 2 * T).rearrange("p (a t) -> p a t", a=2)
    ktok = wk(off["kt"], 6 * 256).rearrange("p (c e) -> p c e", c=6)
    vtok = wk(off["vt"], 6 * 257).rearrange("p (c e) -> p c e", c=6)
    vws = wk(off["vws"], 2 * 257).rearrange("p (c e) -> p c e", c=2)
    c0 = wk(off["c0"], C0RING * 512).rearrange("p (b i d) -> p b i d", b=C0RING, i=2)
    c0t = wk(off["c0t"], 512).rearrange("p (j e) -> p j e", j=2)
    hti = wk(off["hti"], 256).rearrange("p (i t) -> p i t", i=2)
    pt = wk(off["pt"], 2 * P).rearrange("p (b t) -> p b t", b=2)
    bcm, bcw = wk(off["bc"], T), wk(off["bc"] + T, T)
    ct = wk(off["ct"], 2 * 257).rearrange("p (j e) -> p j e", j=2)
    PL = PAD + TP
    UPN = PL + NB * (PAD + LB)
    up = wk(off["up"], 2 * UPN).rearrange("p (a t) -> p a t", a=2)
    ups = up[:, :, PL:UPN].rearrange("p a (b t) -> p a b t", b=NB)
    MG = wk(0, KT * T2).rearrange("p (k t) -> p k t", k=KT)
    sg = wk(off["kt"], 2 * T2).rearrange("p (a t) -> p a t", a=2)
    xtok0 = wk(0, 6 * D).rearrange("p (c e) -> p c e", c=6)
    xtok5 = wk(off["so"], 6 * D).rearrange("p (c e) -> p c e", c=6)
    nqs = wk(off["vn"] + SMP * 257, 2 * TS).rearrange("p (j t) -> p j t", j=2)
    ust = wk(off["vn"], 5 * 256)
    WIN = PAD + LB
    UR = WIN + PAD
    xc = wk(off["c0t"], KT * NB * PAD).rearrange("p (k w) -> p k w", k=KT)
    gcs = wk(off["vt"], KT * T2).rearrange("p (k t) -> p k t", k=KT)
    assert off["c0t"] + KT * NB * PAD <= off["up"] and off["pt"] == off["hti"] + 256
    z0 = off["so"] + 6 * D
    assert z0 + 8 * T <= total
    tmp = [wk(z0 + i * T, T2) for i in range(8)]
    ln = [wk(off["vt"] + KT * T + i * T, T2) for i in range(5)]
    assert off["vt"] + KT * T + 5 * T <= total and off["vt"] - off["kt"] >= 2 * T

    ident, ones, onesd = sb("ident", [P, P]), sb("ones", [P, P]), sb("onesd", [P, 1])
    maskc, maskd, bmask = sb("maskc", [P, P]), sb("maskd", [P, P]), sb("bmask", [P, NB])
    prm = sb("prm", [P, 64])
    cwt = sb("cwt", [P, KT, CONV_W])
    CVF = CV[:, :, :].rearrange("p k t -> p (k t)")
    VEC = ["g_pre_mix", "g_headnorm", "conv_b", "ln_g", "ln_b", "g_post_mix", "g_pre_ffn", "g_post_ffn"]

    def vec(name, kk, n=1):
        o = VEC.index(name) * KT
        return prm[:, bass.ds(o + kk, n)] if not isinstance(kk, int) else prm[:, o + kk:o + kk + n]

    colA = sb("colA", [P, HEADS, 31])
    colH = sb("colH", [P, 31])
    cwu = sb("cwu", [P, 2, CONV_W + 1])
    ghd = sb("ghd", [P, 2])
    wlb = sb("wlb", [NB, HEADS])
    n0t = sb("n0t", [P, 2, NB * HEADS])
    n0b = sb("n0b", [NB, DH])
    wsb = sb("wsb", [P, NB])
    nsel = sb("nsel", [P, 2, NB])
    bst, mv = sb("bst", [P, 6, 6]), sb("mv", [P, 6, 2])
    sm = sb("sm", [P, 48])
    bif = sb("bif", [2 * HEADS, 1])
    mhalf = sb("mhalf", [P, 6])
    rb = off["kt"]

    def row(i):
        return WK[0:HEADS, rb + i * T:rb + (i + 1) * T]

    GI8 = WK[0:2 * HEADS, rb:rb + T]
    r9 = rb + 8 * T
    m0r = WK[0:HEADS, r9:r9 + NB + NPC + 1]
    wlr = WK[0:HEADS, r9 + 16:r9 + 29]
    wld = WK[0:HEADS, r9 + 32:r9 + 84].rearrange("p (h j) -> p h j", h=HEADS)
    assert r9 + 84 <= off["c0t"]

    out = [nc.alloc_psum_tensor(f"out{i}", [P, 2, 512], F32) for i in range(2)]
    BK = [nc.alloc_psum_tensor(f"bank{i}", [P, 512], F32) for i in (4, 5, 6, 7)]
    B4, B5, B6, B7 = BK

    def half(n):
        return HALF if n.base < N_GM0 else HALF2

    def gout(n):
        return out[n.par % 2][:, :, 0:half(n)]

    d_rows = nc.dram_tensor("d_rows", (HEADS, 2, T), F32, kind="Internal").ap()
    d_cache = nc.dram_tensor("d_cache", (P, KT, NB * PAD), F32, kind="Internal").ap()

    S = {}

    def sem(name):
        if name not in S:
            S[name] = nc.alloc_semaphore(name)
        return S[name]

    def wait(e, name, v):
        if isinstance(v, int) and v <= 0:
            return
        e.wait_ge(sem(name), v)

    class Chain:

        def __init__(self, e, name):
            self.e = e
            self.start(name)

        def start(self, name, per=0, i=0):
            self.name, self.per, self.i, self.v = name, per, i, 0

        def inc(self, ins):
            ins.then_inc(sem(self.name), 1)
            self.v = self.v + 1

        def wait(self):
            wait(self.e, self.name, self.per * self.i + self.v if self.per else self.v)

        def link(self, ins):
            self.inc(ins)
            self.wait()

    w_in = a["w_in"].rearrange("o (k p) n -> p (o k) n", p=P)
    w_m = a["w_branch_m"].rearrange("o (k p) n -> p (o k) n", p=P)
    w_c = a["w_branch_c"].rearrange("o (k p) n -> p (o k) n", p=P)
    w_o = a["w_out"].rearrange("o (k p) n -> p (o k) n", p=P)
    w_1 = a["w_ff1"].rearrange("o (k p) n -> p (o k) n", p=P)
    w_2 = a["w_ff2"].rearrange("o (k p) n -> p (o k) n", p=P)


    def load_tile(sp, n, w, k0, col, more=0):
        need, at = val(n) - (NSTAGE - 1) + max(more, 0), col
        if n.per:
            need, k0, at = [x if isinstance(x, int) else sp.snap(x) for x in (need, k0, at)]
        src = w[:, k0:k0 + KT, bass.ds(at, P)] if isinstance(k0, int) else w[:, bass.ds(k0, KT), at:at + P]
        if not isinstance(need, int):
            sp.wait_ge(sem(f"ld{n.par}"), 16)
        if more >= 0:
            wait(sp, "w_lo", need)
        sp.dma_start(ST[:, n.par, :, :], src).then_inc(sem(f"ld{n.par}"), 16)

    def split_hi(act, n, par):
        act.wait_ge(sem(f"ld{par % NSTAGE}"), ldcount(n))
        wait(act, "tile_done", val(n) - 1)
        act.activation(WH[:, par % 2, :, :], ST[:, par % NSTAGE, :, :], ACT.Copy).then_inc(sem("w_hi"), 1)

    def split_lo(dve, n, par):
        wait(dve, "w_hi", val(n) + 1)
        dve.tensor_tensor(WL[:, par % 2, :, :], ST[:, par % NSTAGE, :, :],
                          WH[:, par % 2, :, :].bitcast(F32), ALU.subtract).then_inc(sem("w_lo"), 1)

    class N:

        def __init__(self, base, per=0, i=0):
            self.base, self.per, self.i = base, per, i

        def __add__(self, k):
            return N(self.base + k, self.per, self.i)

        @property
        def par(self):
            return self.base % 4

    def val(n):
        return n.base + n.per * n.i if n.per else n.base

    def ldcount(n):
        return 16 * (n.base // NSTAGE + 1) + (16 * n.per // NSTAGE) * n.i if n.per else 16 * (n.base // NSTAGE + 1)

    def ofcount(n):
        return n.base // 2 + (n.per // 2) * n.i if n.per else n.base // 2

    def evacuated(e, n):
        e.wait_ge(sem(f"of{n.par % 2}"), ofcount(n) + 1)

    def gemm(pe, n, xh, xl, gaps=(), rhs_ready=None):
        wait(pe, "w_lo", val(n) + 1)
        wait(pe, f"of{n.par % 2}", ofcount(n))
        s, H, ms = n.par % 2, half(n), []
        for kk in range(KT):
            for w, x in ((WH, xh), (WH, xl), (WL, xh)):
                for h in range(2):
                    ms.append((kk, w, x, h))
        cuts = [len(ms) * (g + 1) // (len(gaps) + 1) for g in range(len(gaps))]
        for m, (kk, w, x, h) in enumerate(ms):
            if m in cuts:
                gaps[cuts.index(m)]()
            if rhs_ready and m % 6 == 0:
                rhs_ready(kk)
            last = pe.matmul(out[s][:, h, 0:H], w[:, s, kk, :], x[:, kk, h * H:(h + 1) * H],
                             start=(m < 2), stop=(m >= len(ms) - 2))
        last.then_inc(sem("tile_done"), 1)

    def o_scaled(kk):
        return (tmp[4], tmp[5], tmp[1], tmp[3])[kk % 4]

    OUTC = [TS + P * j for j in range(4)] + [0]

    with nc.Block() as block:
        @block.sync
        def _(sp):
            def dma(o, i, name, slow=False):
                return sp.dma_start(o, i, allow_slow_non_contiguous=slow).then_inc(sem(name), 16)

            def frames(to, name, first=0):
                for c in range(first, 6):
                    src = (a["meta_tokens"] if c == 0 else a["x_sample"].rearrange("b t d -> (b t) d") if c == SMP
                           else a["x_prompt"][0, P * (c - 1):P * c, :])
                    dma(to[0:CHUNKS[c][1], c, :], src, f"{name}{c}")

            frames(xtok0, "xin")
            for i, nm in enumerate(VEC):
                dma(CVF[KT * i:KT * i + KT, 0:P], a[nm].rearrange("o (k p) -> (o k) p", p=P), "vecs")
            dma(bif[:, :], a["b_if"].rearrange("o h -> h o"), "smalls", True)
            dma(m0r[:, 0:NB], a["state_mlstm_m"].rearrange("o b h -> (o h) b"), "smalls", True)
            load_tile(sp, N(0), w_in, 0, OFF_I)
            dma(CVF[0:CONV_W, P:P + D], a["conv_w"][0], "vecs")
            dma(CVF[0:NB * HEADS, P + D:P + D + DH], a["state_mlstm_n"].rearrange("o b h d -> (o b h) d"), "vecs")
            cache = a["cache_conv"].rearrange("o (g b) w n -> g (o b w) n", g=2)
            for g in range(2):
                dma(CVF[0:4 * PAD, P + D + DH + g * D:P + D + DH + (g + 1) * D], cache[g, :, :], "cache")

            def head_loads(i):
                first = isinstance(i, int)
                n = N(N_HEADS0, PER_HEAD, i)
                cols = [o + x * P for o in (OFF_K, OFF_Q, OFF_V, OFF_O) for x in range(2)]
                cols += [o + x * P for x in range(2) for o in (OFF_CB, OFF_CA)]
                for r, col in enumerate(cols):
                    if r == 7 and first:
                        sp.wait_ge(sem("cache_out"), 16)
                        sp.wait_ge(sem("rows_out"), 32)
                        bc_load(d_rows[0:1, :, :])
                    elif r == 3 and not first:
                        gated = sp.snap(ofcount(n + -1) + 1)
                        tile, src = sp.snap((i - 1) * 2), d_rows[bass.ds(i, 1), :, :]
                        tile1 = sp.snap((i - 1) * 2 + 1)
                        sp.wait_ge(sem("rows_out"), 32)
                        sp.wait_ge(sem(f"of{(n + -1).par % 2}"), gated)
                        bc_load(src)
                        sp.wait_ge(sem("cache_out"), 16)
                        for x, tl in enumerate((tile, tile1)):
                            sp.dma_start(ups[:, x, :, 0:PAD], d_cache[:, bass.ds(tl, 1), :].rearrange(
                                "p o (b w) -> p (o b) w", b=NB)).then_inc(sem("cache_in"), 16)
                    load_tile(sp, n + r, w_in, 0, i * 2 * P + col)

            def bc_load(src):
                sp.dma_start(WK[:, off["bc"]:off["bc"] + 2 * T],
                             src.rearrange("h r t -> h (r t)").to_broadcast([P, 2 * T])).then_inc(sem("bc_in"), 16)

            head_loads(0)
            with sp.Fori(1, HEADS) as i:
                head_loads(i)
            def gates_and_branch(i):
                for r, (w, o) in enumerate(((w_in, OFF_GM), (w_in, OFF_GM + P), (w_m, 0), (w_m, P))):
                    more = 0 if isinstance(i, int) else {1: 1, 2: -1}.get(r, 0)
                    load_tile(sp, N(N_GM0, 4, i) + r, w, 0, i * 2 * P + o, more)

            gates_and_branch(0)
            sp.wait_ge(sem("conv"), 2 * TAPS * 3)
            for x in range(2):
                dma(ups[:, x, :, 0:PAD], d_cache[:, 6 + x, :].rearrange("p (b w) -> p b w", b=NB), "cache_in")
            with sp.Fori(1, KT // 2) as i:
                gates_and_branch(i)
            for n0, w, o in ((N_GC0, w_in, OFF_GC), (N_GC0 + KT, w_c, 0)):
                with sp.Fori(0, 2) as i:
                    for r in range(4):
                        load_tile(sp, N(n0, 4, i) + r, w, 0, i * 4 * P + (o + r * P))
            for r in range(4):
                load_tile(sp, N(N_OUT0 + r), w_o, 0, r * P)
            sp.wait_ge(sem("mg2"), KT)
            frames(xtok5, "xagain", 1)
            for r in range(4, KT):
                load_tile(sp, N(N_OUT0 + r), w_o, 0, r * P)
            with sp.Fori(0, DFF // D) as c:
                n = N(N_FF0, 2 * KT, c)
                for r in range(KT):
                    load_tile(sp, n + r, w_1, 0, c * D + r * P)
                for r in range(KT):
                    load_tile(sp, n + (KT + r), w_2, c * KT, r * P)
            for c in range(5):
                wait(sp, "ytok", c + 1)
                o = a["o_y_sample"].rearrange("b t d -> (b t) d") if c == 4 else a["o_y_prompt"][0, P * c:P * c + P, :]
                dma(o, xtok5[:, c, :], "stores")
            sp.wait_ge(sem("stores"), 16 * 5)

        @block.gpsimd
        def _(g):
            g.memset(ident[:, :], 0.0).then_inc(sem("g_seq"), 1)
            g.memset(maskc[:, :], 0.0).then_inc(sem("g_seq"), 1)
            g.memset(maskd[:, :], 0.0).then_inc(sem("g_seq"), 1)
            g.memset(bmask[:, :], 1.0).then_inc(sem("g_seq"), 1)
            g.memset(mhalf[:, :], -0.5).then_inc(sem("mhalf"), 1)
            g.wait_ge(sem("g_seq"), 4)
            g.affine_select(out=ident[:, :], in_=ident[:, :], compare_op=ALU.not_equal, fill=1.0, base=0,
                            pattern=[[-1, P]], channel_multiplier=1).then_inc(sem("consts"), 1)
            g.affine_select(out=maskc[:, :], in_=maskc[:, :], compare_op=ALU.is_ge, fill=NEG, base=0,
                            pattern=[[1, P]], channel_multiplier=-1).then_inc(sem("consts"), 1)
            md = maskd[:, :].rearrange("p (b t) -> p b t", b=NB)
            g.affine_select(out=maskd[:, :], in_=maskd[:, :], compare_op=ALU.is_ge, fill=NEG, base=0,
                            pattern=[[1, P]], channel_multiplier=-1).then_inc(sem("g_seq"), 1)
            g.wait_ge(sem("g_seq"), 5)
            g.affine_select(out=md, in_=md, compare_op=ALU.is_ge, fill=NEG, base=0,
                            pattern=[[-LB, NB], [0, LB]], channel_multiplier=1).then_inc(sem("consts"), 1)
            g.affine_select(out=bmask[:, :], in_=bmask[:, :], compare_op=ALU.is_ge, fill=0.0, base=0,
                            pattern=[[-LB, NB]], channel_multiplier=1).then_inc(sem("g_seq"), 1)
            g.wait_ge(sem("g_seq"), 6)
            g.affine_select(out=bmask[:, :], in_=bmask[:, :], compare_op=ALU.is_ge, fill=0.0, base=LB - 1,
                            pattern=[[LB, NB]], channel_multiplier=-1).then_inc(sem("consts"), 1)
            g.wait_ge(sem("mhalf"), 1)
            g.wait_ge(sem("ms0"), 1)
            g.tensor_tensor(sm[:, 18:24], sm[:, 6:12], mhalf[:, :], ALU.pow).then_inc(sem("rt0"), 1)
            g.wait_ge(sem("conv"), 2 * TAPS * (HEADS - 1))
            g.wait_ge(sem("of0"), N_GM0 // 2 + 1)
            g.tensor_tensor(ln[0], CV[:, 0, :], CV[:, 1, :], ALU.add).then_inc(sem("csum"), 1)
            for kk in range(2, KT - 2):
                g.wait_ge(sem("csum"), kk - 1)
                g.tensor_tensor(ln[0], ln[0], CV[:, kk, :], ALU.add).then_inc(sem("csum"), 1)
            g.wait_ge(sem("lvar"), 1)
            g.tensor_tensor(sm[:, 6:11], sm[:, 0:5], mhalf[:, 0:5], ALU.pow).then_inc(sem("lrt"), 1)
            g.wait_ge(sem("ovar"), 1)
            g.tensor_tensor(sm[:, 6:11], sm[:, 0:5], mhalf[:, 0:5], ALU.pow).then_inc(sem("ort"), 1)
            g.wait_ge(sem("orr"), 2)
            for kk in range(1, KT, 2):
                wait(g, "x2", kk - 3)
                g.tensor_tensor(o_scaled(kk), CV[:, kk, :], tmp[2], ALU.mult).then_inc(sem("om1"), 1)
            for kk in range(KT):
                g.wait_ge(sem("x2"), kk + 1)
                g.memset(CV[:, kk, :], 0.0).then_inc(sem("y_zero"), 1)
            g.tensor_tensor(tmp[7], MG[:, 0, :], MG[:, 0, :], ALU.mult).then_inc(sem("fsum"), 1)
            for kk in range(1, KT):
                sq = (tmp[0], tmp[6])[kk % 2]
                g.tensor_tensor(sq, MG[:, kk, :], MG[:, kk, :], ALU.mult).then_inc(sem("fsum"), 1)
                g.wait_ge(sem("fsum"), 2 * kk)
                g.tensor_tensor(tmp[7], tmp[7], sq, ALU.add).then_inc(sem("fsum"), 1)
            g.wait_ge(sem("yvar"), 1)
            g.tensor_tensor(sm[:, 36:41], sm[:, 30:35], mhalf[:, 0:5], ALU.pow).then_inc(sem("yrt"), 1)

        @block.scalar
        def _(act):
            def copy(o, i, name, fn=ACT.Copy, **kw):
                act.activation(o, i, fn, **kw).then_inc(sem(name), 1)

            act.wait_ge(sem("v_consts"), 1)
            for c, (_, L) in enumerate(CHUNKS):
                act.wait_ge(sem(f"xin{c}"), 16)
                wait(act, "ss0", c)
                act.activation(out[0][0:L, :, :].rearrange("p h t -> p (h t)"), xtok0[0:L, c, :], ACT.Square,
                               accum_out=sm[0:L, c:c + 1]).then_inc(sem("ss0"), 1)
            act.wait_ge(sem("t_par"), 1)
            copy(prm[:, :], B6[:, 0:64], "prm_ready")
            copy(n0t[:, :, :], B6[:, 64:128].rearrange("p (j b) -> p j b", j=2), "prm_ready")
            copy(cwt[:, :, :], B7[:, 0:KT * CONV_W].rearrange("p (k w) -> p k w", k=KT), "prm_ready")
            act.wait_ge(sem("prm_ready"), 3)
            def hi(n):
                split_hi(act, n, n.par)

            hi(N(0))
            hi(N(1))
            for kk in range(KT):
                act.wait_ge(sem("t_x"), kk + 1)
                copy(XH[:, kk, P0:T], out[kk % 2][:, 0, :], "xh", scale=vec("g_pre_mix", kk))
                copy(XH[:, kk, 0:P0], out[kk % 2][:, 1, 0:P0], "xh", scale=vec("g_pre_mix", kk))

            def evac(n, o, fn=ACT.Copy, **kw):
                act.wait_ge(sem("tile_done"), val(n) + 1)
                act.activation(o, gout(n), fn, **kw).then_inc(sem(f"of{n.par % 2}"), 1)

            def two(ap):
                return ap.rearrange("p (h t) -> p h t", h=2)

            def cache_copies(k0):
                for kk in range(k0, k0 + 4):
                    act.wait_ge(sem("t_cache"), kk + 1)
                    copy(xc[:, kk, :], BK[kk % 4][:, 0:NB * PAD], "cache_sb")

            cache_copies(0)
            act.wait_ge(sem("smalls"), 32)
            act.wait_ge(sem("xl"), 2 * KT)
            act.wait_ge(sem("tile_done"), 1)
            act.activation(two(GI8), gout(N(0))[0:2 * HEADS], ACT.Identity, bias=bif[:, 0:1]).then_inc(sem("of0"), 1)
            act.wait_ge(sem("of0"), 1)
            act.dma_start(row(1), WK[HEADS:2 * HEADS, rb:rb + T]).then_inc(sem("f_rows"), 16)
            cache_copies(4)
            act.wait_ge(sem("cache_sb"), KT)
            act.dma_start(d_cache, xc).then_inc(sem("cache_out"), 16)
            def rows_log():
                act.wait_ge(sem("r_nabs"), 1)
                copy(row(3), row(3), "r_e", ACT.Exp)
                act.wait_ge(sem("r_e"), 1)
                copy(row(4), row(3), "r_ln", ACT.Ln, bias=1.0)
                act.wait_ge(sem("r_ln"), 1)
                copy(row(5), row(4), "r_inv", ACT.Exp, scale=-1.0)

            def rows_exp():
                act.wait_ge(sem("r_args"), 1)
                copy(row(2), row(2), "r_exp", ACT.Exp)
                copy(row(4), row(4), "r_exp", ACT.Exp)
                copy(row(5), row(5), "r_exp", ACT.Exp)
                act.wait_ge(sem("r_exp"), 3)
                act.dma_start(d_rows[:, 0, :], row(6)).then_inc(sem("rows_out"), 16)
                act.dma_start(d_rows[:, 1, :], row(4)).then_inc(sem("rows_out"), 16)
                act.dma_start(a["o_m_prompt"].rearrange("o b h -> (o h) b"), row(7)[:, T - 1:T],
                              allow_slow_non_contiguous=True).then_inc(sem("m_out"), 16)
                act.dma_start(a["o_m_sample"].rearrange("o b h -> (o h) b"), row(7)[:, NMETA + LB - 1:P0:LB],
                              allow_slow_non_contiguous=True).then_inc(sem("m_out"), 16)

            def rows_free():
                act.wait_ge(sem("cols"), 3)
                act.wait_ge(sem("rows_out"), 32)
                act.wait_ge(sem("m_out"), 32)

            def c0_load(i, b):
                wait(act, f"c1_out{b % C0RING}", 16 * ((NB // C0RING) * i + b // C0RING))
                act.dma_start(c0[:, b % C0RING, :, :],
                              a["state_mlstm_C"][0, b, bass.ds(i, 1), :, :].rearrange("o (i p) d -> p (o i) d", p=P)
                              ).then_inc(sem(f"c0_in{b % C0RING}"), 16)

            def c1_store(i, b):
                act.wait_ge(sem("c1"), NB * i + b + 1)
                act.dma_start(a["o_C_sample"][0, b, bass.ds(i, 1), :, :].rearrange("o (i p) d -> p (o i) d", p=P),
                              c0[:, b % C0RING, :, :]).then_inc(sem(f"c1_out{b % C0RING}"), 16)

            def u_rows(i):
                act.wait_ge(sem("t_u"), i + 1)
                copy(ust[0:UR, 0:512], B6[0:UR, :], "u_sb")
                copy(ust[0:UR, 512:1024], B7[0:UR, :], "u_sb")
                copy(ust[0:PAD, 1024:1280], B5[0:PAD, 0:256], "u_sb")
                act.wait_ge(sem("u_sb"), 3 * i + 3)
                for b in range(2):
                    act.dma_start(a["o_conv_sample"].rearrange("o (g b) w n -> b w (o g) n", b=2)[
                                      b, :, :, bass.ds(i * 2 * P, 2 * P)],
                                  ust[b * WIN:b * WIN + PAD, 0:1024].rearrange("p (g n) -> p g n", g=NB // 2)
                                  ).then_inc(sem("u_out"), 16)
                act.dma_start(a["o_conv_prompt"][0, 0, :, bass.ds(i * 2 * P, 2 * P)],
                              ust[0:PAD, 1024:1280]).then_inc(sem("u_out"), 16)

            def epilogue_root(i):
                act.wait_ge(sem("hvar"), i + 1)
                copy(sm[:, 30:36], sm[:, 24:30], "hrt", ACT.Sqrt)

            def epilogue_out(i):
                act.wait_ge(sem("t_ct"), i + 1)
                act.wait_ge(sem("t_int"), NB * i + NB)
                copy(wk(off["c0t"], 512), B7[:, :], "cp_sb")
                act.wait_ge(sem("cp_sb"), i + 1)
                act.dma_start(a["o_C_prompt"][0, 0, bass.ds(i, 1), :, :].rearrange("o (i p) d -> p (o i) d", p=P),
                              wk(off["c0t"], 512).rearrange("p (i d) -> p i d", i=2)).then_inc(sem("cp_out"), 16)
                act.dma_start(a["o_n_prompt"][0, 0, bass.ds(i, 1), :].rearrange("o (j p) -> p (o j)", p=P),
                              ct[:, :, 256], allow_slow_non_contiguous=True).then_inc(sem("np_out"), 16)
                act.wait_ge(sem("hmf"), i + 1)
                copy(GH[:, bass.ds(i * 2, 2), :], qw[:, :, NMETA:T], "hm_hi")

            def tok(i, fill, bank, pair, dst):
                act.wait_ge(sem("t_kv"), 6 * i + fill)
                v = bank[:, 0:512].rearrange("p (c e) -> p c e", c=2)
                if pair == 0:
                    copy(dst[0:NMETA, 0, 0:DH], v[0:NMETA, 0, :], "kv_tok")
                    copy(dst[:, 1, 0:DH], v[:, 1, :], "kv_tok")
                else:
                    copy(dst[:, 2 * pair:2 * pair + 2, 0:DH], v, "kv_tok")

            def values_tok(i):
                tok(i, 4, B5, 0, vtok)
                tok(i, 5, B4, 1, vtok)
                tok(i, 6, B6, 2, vtok)

            def states_in(i):
                wait(act, "n1_out", 16 * i)
                act.dma_start(n0b[:, :], a["state_mlstm_n"][0, :, bass.ds(i, 1), :].rearrange("b o d -> b (o d)")
                              ).then_inc(sem("n0b_in"), 16)
                for b in range(C0RING):
                    c0_load(i, b)

            def exp_weights(i):
                act.wait_ge(sem("wt_arg"), i + 1)
                copy(bcm, bcm, "wt", ACT.Exp)

            def head(i):
                n = N(N_HEADS0, PER_HEAD, i)
                first = isinstance(i, int)
                hi(n + 1)
                if first:
                    rows_log()
                else:
                    epilogue_root(i - 1)
                evac(n, two(k[:, 0, :]), scale=DH ** -0.5)
                hi(n + 2)
                if not first:
                    states_in(i)
                evac(n + 1, two(k[:, 1, :]), scale=DH ** -0.5)
                hi(n + 3)
                if not first:
                    exp_weights(i)
                    epilogue_out(i - 1)
                evac(n + 2, two(q[:, 0, :]))
                hi(n + 4)
                if not first:
                    u_rows(i - 1)
                if first:
                    rows_exp()
                evac(n + 3, two(q[:, 1, :]))
                if not first:
                    tok(i, 1, B4, 0, ktok)
                    tok(i, 2, B5, 1, ktok)
                hi(n + 5)
                wait(act, "u_out", 48 * i)
                evac(n + 4, two(vf[:, 0, :]))
                if not first:
                    tok(i, 3, B4, 2, ktok)
                hi(n + 6)
                evac(n + 5, two(vf[:, 1, :]))
                if first:
                    rows_free()
                    states_in(i)
                    tok(i, 1, B4, 0, ktok)
                    tok(i, 2, B5, 1, ktok)
                hi(n + 7)
                if first:
                    exp_weights(i)
                evac(n + 6, two(so[:, 0, :]), ACT.Sigmoid)
                if first:
                    tok(i, 3, B4, 2, ktok)
                else:
                    values_tok(i)
                hi(n + 8)
                evac(n + 7, two(so[:, 1, :]), ACT.Sigmoid)
                if first:
                    values_tok(i)
                for s in range(NSLOT):
                    if s in (1, 4, 7, 10):
                        hi(n + (8 + (s - 1) // 3 + 1))
                    if s in TR_SLOT:
                        b = TR_SLOT[s]
                        act.wait_ge(sem("t_c0"), NB * i + b + 1)
                        wait(act, "t_int", NB * i + b)
                        if b == 0:
                            wait(act, "cp_out", 16 * i)
                        copy(wk(off["c0t"], 512), B4[:, :], "c0t_ready")
                    if s in NUM_SLOT and NUM_SLOT[s] < NPC:
                        numer(i, NUM_SLOT[s])
                    if s == 11:
                        act.wait_ge(sem("t_int"), NB * i + NB)
                        copy(wk(off["hti"], 256), B5[:, 128:384], "hti")
                    if s in STORE_SLOT:
                        c1_store(i, STORE_SLOT[s])
                    if s in LOAD_SLOT:
                        c0_load(i, LOAD_SLOT[s])
                    if s in (3, 9):
                        r = 8 if s == 3 else 10
                        if r == 8:
                            act.wait_ge(sem("qw_ready"), i + 1)
                        else:
                            evacuated(act, n + 9)
                        evac(n + r, two(bcw), ACT.Sigmoid)
                numer(i, SMP)
                act.wait_ge(sem("n1"), i + 1)
                act.dma_start(a["o_n_sample"][0, :, bass.ds(i, 1), :].rearrange("b o d -> b (o d)"), n0b[:, :]
                              ).then_inc(sem("n1_out"), 16)

            def numer(i, c):
                L = CHUNKS[c][1]
                act.wait_ge(sem("t_num"), 6 * i + c + 1)
                copy(num[0:L, c, :], B6[0:L, 0:257], "num")

            head(0)
            with act.Fori(1, HEADS) as i:
                head(i)

            def gates_m(i):
                n = N(N_GM0, 8, i)
                for g in range(2):
                    for r in range(2):
                        hi(n + (4 * g + r + 1))
                        if i or g:
                            evacuated(act, n + (4 * g - 2 + r))
                        evac(n + (4 * g + r), two(sg[:, r, :]), ACT.Sigmoid)
                        if i == g == r == 0:
                            epilogue_root(HEADS - 1)
                    hi(n + (4 * g + 3))
                    if i == g == 0:
                        epilogue_out(HEADS - 1)
                    hi(n + (4 * g + 4))
                    if i == g == 0:
                        u_rows(HEADS - 1)

            gates_m(0)
            gates_m(1)
            for b in range(C0RING):
                act.wait_ge(sem(f"c1_out{b}"), 16 * HEADS * NB // C0RING)
            act.wait_ge(sem("cp_out"), 16 * HEADS)
            act.wait_ge(sem("u_out"), 16 * 3 * HEADS)
            for r in range(KT):
                hi(N(N_GC0 + r + 1))
                if r == 5:
                    act.wait_ge(sem("t_lr"), 1)
                    copy(ln[0][:, TS:T2], B6[:, :], "lr")
                    copy(ln[0][:, 0:TS], B7[:, 0:TS], "lr")
                if r == 3:
                    for kk in range(KT):
                        act.wait_ge(sem("cvc"), kk + 1)
                        wait(act, "lsq", kk - 1)
                        copy(ln[2 + kk % 2], CV[:, kk, :], "csq", ACT.Square)
                if r >= 6:
                    for kk in range(4 * (r - 6), 4 * (r - 5)):
                        act.wait_ge(sem("cvn"), kk + 1)
                        copy(CV[:, kk, :], CV[:, kk, :], "cs", ACT.Silu, scale=vec("ln_g", kk), bias=vec("ln_b", kk))
                        act.wait_ge(sem("cs"), kk + 1)
                        copy(GH[:, kk, :], CV[:, kk, :], "ch")
                evac(N(N_GC0 + r), two(gcs[:, r, :]), ACT.Sigmoid)
                if r == 1:
                    act.wait_ge(sem("t_ln"), 1)
                    copy(ln[1][:, TS:T2], B4[:, :], "mean", scale=1.0 / D)
                    copy(ln[1][:, 0:TS], B5[:, 0:TS], "mean", scale=1.0 / D)
            for r in range(KT):
                hi(N(N_GC0 + KT + r + 1))
                act.wait_ge(sem("mg2"), r + 1)
                copy(XH2[:, r, :], MG[:, r, :], "mh")
            for r in range(KT):
                n = N(N_OUT0 + r)
                hi(n + 1)
                act.wait_ge(sem("tile_done"), val(n) + 1)
                wait(act, "oacc", r - 1)
                act.activation(two(tmp[r % 2]), gout(n), ACT.Square).then_inc(sem("osq"), 1)
                evac(n, two(CV[:, r, :]), scale=vec("g_post_mix", r))
                for x in [0, 1] if r == 1 else [r] if r else []:
                    act.wait_ge(sem("t_xa"), x + 1)
                    act.wait_ge(sem("ml"), x + 1)
                    b0, b1 = (B4, B5) if x % 2 == 0 else (B6, B7)
                    copy(MG[:, x, TS:T2], b0[:, :], "xa")
                    copy(MG[:, x, 0:TS], b1[:, 0:TS], "xa")
            act.wait_ge(sem("t_or"), 1)
            copy(tmp[2][:, TS:T2], B6[:, :], "orr")
            copy(tmp[2][:, 0:TS], B7[:, 0:TS], "orr")
            for kk in range(KT):
                act.wait_ge(sem("x2"), kk + 1)
                copy(XH2[:, kk, :], MG[:, kk, :], "fh", scale=vec("g_pre_ffn", kk))

            def y_frames(r):
                act.wait_ge(sem("t_y"), r + 1)
                copy(CV[:, r, 0:4 * P], B4[:, :], "yt")
                copy(CV[:, r, 4 * P:5 * P], B5[:, 0:P], "yt")

            def ffn(c, last=False):
                n = N(N_FF0, 2 * KT, c)
                for r in range(KT):
                    hi(n + (r + 1))
                    evac(n + r, two(tmp[4 + r % 2]), ACT.Relu)
                    act.wait_ge(sem("hsq"), c * KT + (r + 1))
                    copy(GH[:, r, :], tmp[2 + r % 2], "hh")
                    if last:
                        act.wait_ge(sem("t_x2"), r + 1)
                        copy(xtok5[:, 0:4, r * P:r * P + P], B6[:, :].rearrange("p (c e) -> p c e", c=4), "x2t")
                        copy(xtok5[:, 4, r * P:r * P + P], B7[:, 0:P], "x2t")
                for r in range(KT):
                    if not last or r < KT - 1:
                        hi(n + (KT + 1 + r))
                    if last:
                        wait(act, "yacc", r - 1)
                        evacuated(act, n + (KT + r))
                        copy(tmp[r % 2], CV[:, r, :], "ysq", ACT.Square)
                        copy(CV[:, r, :], CV[:, r, :], "yg", scale=vec("g_post_ffn", r))
                        if r:
                            y_frames(r - 1)

            with act.Fori(0, DFF // D - 1) as c:
                ffn(c)
            ffn(DFF // D - 1, last=True)
            y_frames(KT - 1)
            act.wait_ge(sem("cache_out"), 16)
            act.wait_ge(sem("np_out"), 16 * HEADS)
            act.wait_ge(sem("n1_out"), 16 * HEADS)

        @block.vector
        def _(dve):
            V = Chain(dve, "v_seq")

            def two(ap):
                return ap.rearrange("p (h t) -> p h t", h=2)

            def lo(n):
                split_lo(dve, n, n.par)

            def tt(o, x, y, op):
                return dve.tensor_tensor(o, x, y, op)

            def stt(o, x, s, y, op0, op1):
                return dve.scalar_tensor_tensor(o, x, s, y, op0, op1)

            dve.memset(sm[:, :], 0.0)
            dve.memset(bst[:, :, :], 0.0)
            dve.memset(mv[:, :, :], 0.0)
            dve.memset(colA[:, :, :], 0.0)
            dve.memset(onesd[:, :], 1.0)
            V.link(dve.memset(up[:, :, 0:PAD], 0.0))
            dve.memset(ones[:, :], 1.0).then_inc(sem("v_consts"), 1)
            dve.wait_ge(sem("ss0"), 6)
            dve.tensor_scalar(sm[:, 6:12], sm[:, 0:6], 1.0 / D, EPS, ALU.mult, ALU.add).then_inc(sem("ms0"), 1)
            dve.wait_ge(sem("rt0"), 1)
            for c, (_, L) in enumerate(CHUNKS):
                dve.tensor_scalar(xtok0[0:L, c, :], xtok0[0:L, c, :], sm[0:L, 18 + c:19 + c], None,
                                  ALU.mult).then_inc(sem("xs"), 1)
            lo(N(0))
            lo(N(1))
            dve.wait_ge(sem("prm_ready"), 3)
            for kk in range(KT):
                for h, (p0, cols) in enumerate(((out[kk % 2][:, 0, :], slice(P0, T)),
                                                (out[kk % 2][:, 1, 0:P0], slice(0, P0)))):
                    dve.wait_ge(sem("xh"), 2 * kk + h + 1)
                    stt(XL[:, kk, cols], p0, vec("g_pre_mix", kk), XH[:, kk, cols].bitcast(F32),
                        ALU.mult, ALU.subtract).then_inc(sem("xl"), 1)
            def rows_b():
                dve.wait_ge(sem("f_rows"), 16)
                V.link(dve.tensor_scalar(row(2), row(1), 0.0, None, ALU.min))
                stt(row(3), row(2), 2.0, row(1), ALU.mult, ALU.subtract).then_inc(sem("r_nabs"), 1)
                dve.wait_ge(sem("r_e"), 1)
                V.link(dve.tensor_scalar(row(6), row(3), 1.0, None, ALU.add))
                V.link(dve.tensor_scalar(row(6), row(6), -1.0, None, ALU.add))
                V.link(tt(row(6), row(3), row(6), ALU.subtract))
                dve.wait_ge(sem("r_inv"), 1)
                V.link(tt(row(6), row(6), row(5), ALU.mult))
                V.link(tt(row(6), row(6), row(4), ALU.add))
                V.link(tt(row(2), row(2), row(6), ALU.subtract))
                lo(N(N_HEADS0 + 2))
                V.link(dve.memset(row(6), 1.0))
                V.link(dve.memset(row(6)[:, 0:P0:LB], 0.0))
                V.link(dve.memset(row(6)[:, P0:T:P], 0.0))
                V.link(dve.tensor_tensor_scan(row(1), row(6), row(2), 0.0, ALU.mult, ALU.add))
                V.link(tt(row(0), row(0), row(1), ALU.subtract))
                V.link(dve.memset(row(7), 0.0))
                V.link(dve.memset(m0r[:, NB:NB + 1], 0.0))
                dve.wait_ge(sem("smalls"), 32)

            def rows_max():
                for c, (c_, L) in enumerate(CHUNKS[:NPC]):
                    cs = slice(c_, c_ + L)
                    e_ = slice(c_ + L - 1, c_ + L)
                    m0 = m0r[:, NB + c:NB + c + 1]
                    V.link(dve.tensor_tensor_scan(row(3)[:, cs], row(7)[:, cs], row(0)[:, cs], m0, ALU.add, ALU.max))
                    V.link(tt(m0r[:, NB + c + 1:NB + c + 2], row(3)[:, e_], row(1)[:, e_], ALU.add))
                lo(N(N_HEADS0 + 4))
                for b in range(NB):
                    cs = slice(NMETA + LB * b, NMETA + LB * b + LB)
                    V.inc(dve.tensor_tensor_scan(row(3)[:, cs], row(7)[:, cs], row(0)[:, cs], m0r[:, b:b + 1],
                                                 ALU.add, ALU.max))
                V.wait()
                for c_, L, n_, x in ((0, NMETA, 1, NB), (NMETA, LB, NB, 0), (P0, P, NPC - 1, NB + 1)):
                    v = [row(y)[:, c_:c_ + n_ * L].rearrange("h (b t) -> h b t", b=n_) for y in (4, 3, 2, 0)]
                    V.inc(tt(v[0], m0r[:, x:x + n_].unsqueeze(2).to_broadcast([HEADS, n_, L]), v[1], ALU.subtract))
                    V.inc(tt(v[2], v[3], v[1][:, :, L - 1:L].to_broadcast([HEADS, n_, L]), ALU.subtract))
                V.link(tt(row(7), row(1), row(3), ALU.add))
                V.link(dve.tensor_scalar(row(5), row(7), -1.0, None, ALU.mult))
                dve.tensor_scalar(row(6), row(3), -1.0, None, ALU.mult).then_inc(sem("r_args"), 1)

            def rows_last():
                dve.wait_ge(sem("r_exp"), 3)
                V.link(dve.tensor_copy(wlr[:, 0:1], row(4)[:, NMETA - 1:NMETA]))
                V.link(dve.tensor_copy(wlr[:, 1:NPC], row(4)[:, P0 + P - 1:T:P]))
                V.link(dve.tensor_copy(wlr[:, NPC:13], row(4)[:, NMETA + LB - 1:P0:LB]))
                dve.wait_ge(sem("consts"), 4)
                tt(wld[:, :, :], wlr[:, :].unsqueeze(1).to_broadcast([HEADS, HEADS, 13]),
                   ident[0:HEADS, 0:HEADS].unsqueeze(2).to_broadcast([HEADS, HEADS, 13]), ALU.mult).then_inc(sem("wld"), 1)

            def rows_columns():
                dve.wait_ge(sem("t_cols"), 1)
                dve.tensor_copy(colA[0:NMETA, :, 0:3], B4[0:NMETA, 0:12].rearrange("p (x h) -> p h x", h=HEADS)
                                ).then_inc(sem("cols"), 1)
                dve.tensor_copy(colA[:, :, 3:18], B4[:, 12:72].rearrange("p (x h) -> p h x", h=HEADS)
                                ).then_inc(sem("cols"), 1)
                V.inc(dve.tensor_copy(wlb[:, :], B5[0:NB, 64:64 + HEADS]))
                dve.tensor_copy(colA[:, :, 18:31], B5[:, 0:52].rearrange("p (h j) -> p h j", h=HEADS)
                                ).then_inc(sem("cols"), 1)
                dve.wait_ge(sem("cols"), 3)
                dve.wait_ge(sem("rows_out"), 32)
                dve.wait_ge(sem("m_out"), 32)
                V.link(dve.memset(vtok[:, :, DH:DH + 1], 1.0))

            def taps(u, y0, y1):
                for y in range(y0, min(y1, TAPS)):
                    x, t = divmod(y, CONV_W)
                    for part in range(2):
                        if part == 0:
                            src = up[:, x, NMETA + t:NMETA + t + SEQ]
                            dst = CV[:, bass.ds(u * 2 + x, 1), TS:T2].rearrange("p o t -> p (o t)")
                        else:
                            src = ups[:, x, :, t:t + LB]
                            dst = CV[:, bass.ds(u * 2 + x, 1), 0:TS].rearrange("p o (b t) -> p (o b) t", b=NB)
                        if t == 0:
                            dve.tensor_scalar(dst, src, cwu[:, x, 0:1], cwu[:, x, CONV_W:CONV_W + 1],
                                              ALU.mult, ALU.add).then_inc(sem("conv"), 1)
                        else:
                            wait(dve, "conv", 2 * TAPS * u + (2 * y + part - 1))
                            stt(dst, src, cwu[:, x, t:t + 1], dst, ALU.mult, ALU.add).then_inc(sem("conv"), 1)
                return min(y1, TAPS)

            def unit_params(u):
                V.inc(dve.tensor_copy(cwu[:, :, 0:CONV_W], cwt[:, bass.ds(u * 2, 2), :]))
                V.inc(dve.tensor_copy(cwu[:, :, CONV_W], vec("conv_b", u * 2, 2)))
                V.link(dve.tensor_copy(ghd[:, :], vec("g_headnorm", u * 2, 2)))

            def epilogue_norm(i):
                den, mean, var = num[:, :, DH], mv[:, :, 0], mv[:, :, 1]
                emin = colH[:, 2:18:3]
                dve.wait_ge(sem("num"), 6 * i + 6)
                V.link(stt(sm[:, 18:24], den, -1.0, den, ALU.mult, ALU.max))
                V.inc(tt(sm[:, 18:24], sm[:, 18:24], emin, ALU.max))
                for c, (_, L) in enumerate(CHUNKS):
                    V.inc(dve.bn_aggr(mv[0:L, c, :], bst[0:L, c, :]))
                V.wait()
                V.link(dve.reciprocal(sm[:, 36:42], sm[:, 18:24]))
                V.link(tt(sm[:, 18:24], var, sm[:, 36:42], ALU.mult))
                V.link(tt(sm[:, 18:24], sm[:, 18:24], sm[:, 36:42], ALU.mult))
                dve.tensor_scalar(sm[:, 24:30], sm[:, 18:24], EPS, None, ALU.add).then_inc(sem("hvar"), 1)
                dve.wait_ge(sem("hrt"), i + 1)
                V.link(dve.reciprocal(sm[:, 18:24], sm[:, 30:36]))
                V.link(tt(sm[:, 36:42], sm[:, 36:42], sm[:, 18:24], ALU.mult))
                V.link(stt(sm[:, 42:48], mean, -1.0, sm[:, 36:42], ALU.mult, ALU.mult))
                for c, (_, L) in enumerate(CHUNKS):
                    dve.tensor_scalar(num[0:L, c, 0:DH], num[0:L, c, 0:DH], sm[0:L, 36 + c:37 + c],
                                      sm[0:L, 42 + c:43 + c], ALU.mult, ALU.add).then_inc(sem("hn"), 1)
                dve.wait_ge(sem("hn"), 6 * i + 6)

            def epilogue_gate(i):
                dve.wait_ge(sem("t_ht"), i + 1)
                for x in range(2):
                    stt(qw[:, x, P0:T], (B4, B5)[x][:, :], ghd[:, x:x + 1], so[:, x, P0:T],
                        ALU.mult, ALU.mult)
                for x in range(2):
                    ins = stt(qw[:, x, NMETA:P0], B6[:, x * TS:(x + 1) * TS],
                              ghd[:, x:x + 1], so[:, x, NMETA:P0], ALU.mult, ALU.mult)
                ins.then_inc(sem("hmf"), 1)
                dve.wait_ge(sem("hm_hi"), i + 1)
                tt(GL[:, bass.ds(i * 2, 2), :], qw[:, :, NMETA:T], GH[:, bass.ds(i * 2, 2), :].bitcast(F32),
                   ALU.subtract).then_inc(sem("hm_lo"), 1)

            def head_params(i):
                V.inc(dve.tensor_copy(colH[:, :], colA[:, bass.ds(i, 1), :].rearrange("p o x -> p (o x)")))
                V.link(dve.tensor_copy(nsel[:, :, :], n0v(i)))
                V.link(dve.tensor_scalar(wsb[:, :], bmask[:, :], colH[:, 3 * SMP + 1:3 * SMP + 2], None, ALU.mult))

            def n0v(i):
                return n0t[:, :, :].rearrange("p j (b h) -> p h j b", h=HEADS)[:, bass.ds(i, 1), :, :].rearrange(
                    "p o j b -> p (o j) b")

            def scores_weights(i):
                dve.wait_ge(sem("bc_in"), 16 * (i + 1))
                for c, (c_, L) in enumerate(CHUNKS):
                    mask = maskd if c == SMP else maskc
                    ins = stt(bcm[0:L, c_:c_ + L], bcm[0:L, c_:c_ + L], colH[0:L, 3 * c:3 * c + 1], mask[0:L, 0:L],
                              ALU.add, ALU.add)
                ins.then_inc(sem("wt_arg"), 1)

            def vws_next(i, u):
                kind, c = UPDATES[u]
                wait(dve, "t_upd", NUPD * i + u - 1)
                if kind == "U":
                    L = CHUNKS[c][1]
                    dve.tensor_scalar(vws[0:L, u % 2, :], vtok[0:L, c, :], colH[0:L, 3 * c + 1:3 * c + 2], None,
                                      ALU.mult).then_inc(sem("vws"), 1)
                else:
                    dve.tensor_scalar(vws[:, u % 2, :], vtok[:, SMP, :], wsb[:, c:c + 1], None,
                                      ALU.mult).then_inc(sem("vws"), 1)

            def update(i, u):
                kind, c = UPDATES[u]
                dve.wait_ge(sem("t_upd"), NUPD * i + u + 1)
                psum = B7[:, :].rearrange("p (j e) -> p j e", j=2)
                if kind == "D":
                    slot = c % C0RING
                    dve.wait_ge(sem(f"c0_in{slot}"), 16 * ((NB // C0RING) * i + c // C0RING + 1))
                    stt(c0[:, slot, :, :], c0[:, slot, :, :], colH[:, 23 + c:24 + c], psum, ALU.mult,
                        ALU.add).then_inc(sem("c1"), 1)
                elif c == 0:
                    wait(dve, "np_out", 16 * i)
                    dve.tensor_copy(ct[:, :, DH], B5[:, 384:386])
                    dve.tensor_copy(ct[:, :, 0:DH], psum).then_inc(sem("ct_ready"), 1)
                else:
                    dve.wait_ge(sem("ct_ready"), NPC * i + c)
                    stt(ct[:, :, DH], ct[:, :, DH], colH[:, 18 + c:19 + c], B5[:, 384:386], ALU.mult, ALU.add)
                    stt(ct[:, :, 0:DH], ct[:, :, 0:DH], colH[:, 18 + c:19 + c], psum, ALU.mult,
                        ALU.add).then_inc(sem("ct_ready"), 1)

            def stats(i, c):
                L = CHUNKS[c][1]
                dve.wait_ge(sem("num"), 6 * i + c + 1)
                V.inc(dve.bn_stats(bst[0:L, c, :], num[0:L, c, 0:DH]))

            def conv_input(i, r, x, n):
                dve.wait_ge(sem("tile_done"), val(n + r) + 1)
                evacuated(dve, n + (r - 1))
                wait(dve, "conv", 2 * TAPS * (i - 1) + (TAPS if x == 0 else 2 * TAPS))
                wait(dve, "t_u", i)
                p0 = gout(n + r)
                tt(ups[:, x, :, PAD:PAD + LB], p0[:, 0, NMETA:P0].rearrange("p (b t) -> p b t", b=NB),
                   bcw[:, NMETA:P0].rearrange("p (b t) -> p b t", b=NB), ALU.mult)
                tt(up[:, x, PAD:PAD + NMETA], p0[:, 0, 0:NMETA], bcw[:, 0:NMETA], ALU.mult)
                tt(up[:, x, PAD + NMETA:PAD + HALF - TS], p0[:, 0, P0:HALF], bcw[:, P0:HALF], ALU.mult)
                tt(up[:, x, PAD + HALF - TS:PL], p0[:, 1, :], bcw[:, HALF:T], ALU.mult
                   ).then_inc(sem(f"of{(n + r).par % 2}"), 1)

            def vws_first(i):
                dve.wait_ge(sem("kv_tok"), 8 * i + 8)
                vws_next(i, 0)
                vws_next(i, 1)

            def weigh_q(i):
                tt(qw, q, bcw.unsqueeze(1).to_broadcast([P, 2, T]), ALU.mult).then_inc(sem("qw_ready"), 1)
                dve.wait_ge(sem("qw_ready"), i + 1)

            def head(i):
                first = isinstance(i, int)
                n = N(N_HEADS0, PER_HEAD, i)
                lo(n + 1)
                if first:
                    rows_b()
                    lo(n + 3)
                    rows_max()
                    rows_last()
                    lo(n + 5)
                    rows_columns()
                    head_params(i)
                    lo(n + 6)
                    scores_weights(i)
                    evacuated(dve, n + 3)
                    weigh_q(i)
                    lo(n + 7)
                    lo(n + 8)
                else:
                    epilogue_norm(i - 1)
                    head_params(i)
                    lo(n + 2)
                    unit_params(i - 1)
                    scores_weights(i)
                    lo(n + 3)
                    epilogue_gate(i - 1)
                    dve.wait_ge(sem("cache_in"), 32 * i)
                    t = 0
                    for r in range(2, 8):
                        if r > 2:
                            lo(n + (r + 1))
                        if r == 3:
                            evacuated(dve, n + 3)
                            dve.wait_ge(sem("hm_lo"), i)
                            weigh_q(i)
                        if r == 7:
                            vws_first(i)
                        t = taps(i - 1, t, t + CONV_TILE[r])
                if first:
                    vws_first(i)
                u = 0
                for s in range(NSLOT):
                    if s in (1, 4, 7, 10):
                        lo(n + (8 + (s - 1) // 3 + 1))
                    if s in S_SLOT:
                        c = S_SLOT[s]
                        c_, L = CHUNKS[c]
                        dve.wait_ge(sem("t_s"), 6 * i + c + 1)
                        wait(dve, "t_num", 6 * i + c - 1)
                        if c == 0:
                            dve.wait_ge(sem("wt"), i + 1)
                        tt(pt[0:L, c % 2, 0:L], B5[0:L, 0:L], bcm[0:L, c_:c_ + L], ALU.mult).then_inc(sem("p_ready"), 1)
                    for kind in ("U", "D"):
                        if u < NUPD and UPDATES[u][0] == kind and (
                                (kind == "U" and NUM_SLOT.get(s) == UPDATES[u][1]) or
                                (kind == "D" and UPD_SLOT.get(s) == UPDATES[u][1])):
                            update(i, u)
                            if u + 2 < NUPD:
                                vws_next(i, u + 2)
                            u += 1
                    if s == 9:
                        tt(nqs.rearrange("p j (b t) -> p j b t", b=NB),
                           qw[:, :, NMETA:P0].rearrange("p j (b t) -> p j b t", b=NB),
                           nsel[:, :, :].unsqueeze(3).to_broadcast([P, 2, NB, LB]), ALU.mult).then_inc(sem("nq"), 1)
                    if s == 11:
                        dve.wait_ge(sem("t_n1"), i + 1)
                        dve.wait_ge(sem("n0b_in"), 16 * (i + 1))
                        wait(dve, "n1_out", 16 * i)
                        stt(n0b[:, :], n0b[:, :], wlb[:, bass.ds(i, 1)], B6[0:NB, 0:DH], ALU.mult,
                            ALU.add).then_inc(sem("n1"), 1)
                    if s in NUM_SLOT and NUM_SLOT[s] in (0, 1, 2, 3, 4):
                        stats(i, NUM_SLOT[s])
                    if not first and s in CONV_SLOT:
                        t = taps(i - 1, t, t + CONV_SLOT[s])
                    if s == 6:
                        conv_input(i, 9, 0, n)
                    if s == 12:
                        conv_input(i, 11, 1, n)
                stats(i, SMP)

            head(0)
            with dve.Fori(1, HEADS) as i:
                V.start("v_head", V_HEAD, i - 1)
                head(i)
                assert V.v == V_HEAD, V.v
            V.start("v_after")

            t = 0
            for j in range(2 * KT):
                n = N(N_GM0 + j)
                lo(n + 1)
                if j == 0:
                    epilogue_norm(HEADS - 1)
                if j == 1:
                    unit_params(HEADS - 1)
                    epilogue_gate(HEADS - 1)
                    dve.wait_ge(sem("cache_in"), 32 * HEADS)
                if j == 10:
                    dve.wait_ge(sem("u_out"), 48 * HEADS)
                if j % 4 >= 2:
                    kk = 2 * (j // 4) + j % 2
                    dve.wait_ge(sem("tile_done"), val(n) + 1)
                    evacuated(dve, n + -2)
                    tt(two(MG[:, kk, :]), gout(n), two(sg[:, j % 2, :]), ALU.mult
                       ).then_inc(sem(f"of{n.par % 2}"), 1)
                if j >= 1:
                    t = taps(HEADS - 1, t, t + 5)
            assert t == TAPS
            def conv_remainders(k0, k1):
                for kk in range(k0, k1):
                    dve.wait_ge(sem("ch"), kk + 1)
                    tt(GL[:, kk, :], CV[:, kk, :], GH[:, kk, :].bitcast(F32), ALU.subtract).then_inc(sem("cl"), 1)

            dve.wait_ge(sem("np_out"), 16 * HEADS)
            for r in range(KT):
                lo(N(N_GC0 + r + 1))
                if r == 0:
                    dve.wait_ge(sem("conv"), 2 * TAPS * HEADS)
                    dve.wait_ge(sem("csum"), KT - 3)
                    V.link(tt(ln[0], ln[0], CV[:, KT - 2, :], ALU.add))
                    tt(ln[0], ln[0], CV[:, KT - 1, :], ALU.add).then_inc(sem("lsum"), 1)
                if r == 2:
                    dve.wait_ge(sem("mean"), 2)
                    for kk in range(KT):
                        tt(CV[:, kk, :], CV[:, kk, :], ln[1], ALU.subtract).then_inc(sem("cvc"), 1)
                if r == 3:
                    for kk in range(KT):
                        dve.wait_ge(sem("csq"), kk + 1)
                        if kk == 0:
                            dve.tensor_copy(ln[4], ln[2]).then_inc(sem("lsq"), 1)
                        else:
                            dve.wait_ge(sem("lsq"), kk)
                            tt(ln[4], ln[4], ln[2 + kk % 2], ALU.add).then_inc(sem("lsq"), 1)
                if r == 5:
                    dve.wait_ge(sem("t_ln"), 2)
                    dve.tensor_scalar(sm[:, 0:5], B4[:, 0:5], 1.0 / D, EPS, ALU.mult, ALU.add).then_inc(sem("lvar"), 1)
                    dve.wait_ge(sem("lr"), 2)
                    for kk in range(KT):
                        tt(CV[:, kk, :], CV[:, kk, :], ln[0], ALU.mult).then_inc(sem("cvn"), 1)
                if r >= 6:
                    conv_remainders(4 * (r - 6), 4 * (r - 5))
            for r in range(KT):
                n = N(N_GC0 + KT + r)
                lo(n + 1)
                dve.wait_ge(sem("tile_done"), val(n) + 1)
                evacuated(dve, N(N_GC0 + r))
                tt(two(ln[r % 2]), gout(n), two(gcs[:, r, :]), ALU.mult).then_inc(sem(f"of{n.par % 2}"), 1)
                evacuated(dve, n)
                tt(MG[:, r, :], MG[:, r, :], ln[r % 2], ALU.add).then_inc(sem("mg2"), 1)
                dve.wait_ge(sem("mh"), r + 1)
                tt(XL2[:, r, :], MG[:, r, :], XH2[:, r, :].bitcast(F32), ALU.subtract).then_inc(sem("ml"), 1)

            def add_up(sq, name, acc, kk):
                dve.wait_ge(sem(sq), kk + 1)
                if kk == 0:
                    dve.tensor_copy(acc, tmp[0]).then_inc(sem(name), 1)
                else:
                    dve.wait_ge(sem(name), kk)
                    tt(acc, acc, tmp[kk % 2], ALU.add).then_inc(sem(name), 1)

            for r in range(KT):
                lo(N(N_OUT0 + r + 1))
                add_up("osq", "oacc", tmp[6], r)
            dve.wait_ge(sem("t_os"), 1)
            dve.tensor_scalar(sm[:, 0:5], B4[:, 0:5], 1.0 / D, EPS, ALU.mult, ALU.add).then_inc(sem("ovar"), 1)
            dve.wait_ge(sem("orr"), 2)
            for kk in range(KT + 2):
                if kk < KT and kk % 2 == 0:
                    tt(o_scaled(kk), CV[:, kk, :], tmp[2], ALU.mult).then_inc(sem("om0"), 1)
                if 0 < kk <= KT:
                    x = kk - 1
                    dve.wait_ge(sem("xa"), 2 * x + 2)
                    dve.wait_ge(sem(f"om{x % 2}"), x // 2 + 1)
                    tt(MG[:, x, :], o_scaled(x), MG[:, x, :], ALU.add).then_inc(sem("x2"), 1)
                if kk > 1:
                    x = kk - 2
                    dve.wait_ge(sem("fh"), x + 1)
                    stt(XL2[:, x, :], MG[:, x, :], vec("g_pre_ffn", x), XH2[:, x, :].bitcast(F32),
                        ALU.mult, ALU.subtract).then_inc(sem("fl"), 1)

            def ffn_factors():
                dve.wait_ge(sem("t_fs"), 1)
                V.link(dve.tensor_scalar(sm[:, 12:17], B5[:, 0:5], 1.0 / D, EPS, ALU.mult, ALU.add))
                V.link(dve.reciprocal(sm[:, 18:23], sm[:, 12:17]))
                V.link(stt(sm[:, 24:29], sm[:, 18:23], 1.0 / D, sm[:, 18:23], ALU.mult, ALU.mult))

            def ffn(c, last=False):
                n = N(N_FF0, 2 * KT, c)
                for r in range(KT):
                    lo(n + (r + 1))
                    evacuated(dve, n + r)
                    tt(tmp[2 + r % 2], tmp[4 + r % 2], tmp[4 + r % 2], ALU.mult).then_inc(sem("hsq"), 1)
                    dve.wait_ge(sem("hh"), c * KT + (r + 1))
                    tt(GL[:, r, :], tmp[2 + r % 2], GH[:, r, :].bitcast(F32), ALU.subtract).then_inc(sem("hl"), 1)
                for r in range(KT):
                    if not last or r < KT - 1:
                        lo(n + (KT + 1 + r))
                    if last and r > 0:
                        add_up("ysq", "yacc", tmp[6], r - 1)
                    dve.wait_ge(sem("tile_done"), val(n + (KT + r)) + 1)
                    dve.wait_ge(sem("y_zero"), r + 1)
                    tt(two(CV[:, r, :]), gout(n + (KT + r)), two(CV[:, r, :]), ALU.add
                       ).then_inc(sem(f"of{(n + r).par % 2}"), 1)

            with dve.Fori(0, DFF // D - 1) as c:
                ffn(c)
            ffn_factors()
            ffn(DFF // D - 1, last=True)
            add_up("ysq", "yacc", tmp[6], KT - 1)
            dve.wait_ge(sem("t_ys"), 1)
            V.link(tt(sm[:, 30:35], B7[:, 0:5], sm[:, 24:29], ALU.mult))
            dve.tensor_scalar(sm[:, 30:35], sm[:, 30:35], EPS, None, ALU.add).then_inc(sem("yvar"), 1)
            dve.wait_ge(sem("yrt"), 1)
            V.link(tt(sm[:, 42:47], sm[:, 36:41], sm[:, 18:23], ALU.mult))
            dve.wait_ge(sem("yt"), 2 * KT)
            for j in range(5):
                to = xtok5[:, j, :].rearrange("p (k e) -> p k e", k=KT)
                stt(to, CV[:, :, j * P:j * P + P], sm[:, 42 + j:43 + j], to, ALU.mult, ALU.add
                    ).then_inc(sem("ytok"), 1)

        @block.tensor
        def _(pe):
            def tr(o, i, name=None):
                r = i.shape[0]
                ins = pe.transpose(o, i, ident[0:r, 0:r])
                if name:
                    ins.then_inc(sem(name), 1)

            def mm(o, l, r, start=True, stop=True):
                return pe.matmul(o, l, r, start=start, stop=stop)

            pe.wait_ge(sem("consts"), 4)
            pe.wait_ge(sem("v_consts"), 1)
            pe.wait_ge(sem("vecs"), 16 * (len(VEC) + 2))
            tr(B6[:, 0:64], CVF[0:64, 0:P])
            for j in range(2):
                tr(B6[:, 64 + 32 * j:96 + 32 * j], CVF[0:32, P + D + P * j:P + D + P * j + P])
            for kk in range(KT):
                tr(B7[:, CONV_W * kk:CONV_W * kk + CONV_W], CVF[0:CONV_W, P + P * kk:2 * P + P * kk],
                   "t_par" if kk == KT - 1 else None)
            def cache_by_channel(k0):
                for kk in range(k0, k0 + 4):
                    wait(pe, "cache_sb", kk - 3)
                    for g in range(2):
                        o = P + D + DH + g * D + kk * P
                        tr(BK[kk % 4][:, g * 4 * PAD:(g + 1) * 4 * PAD], CVF[0:4 * PAD, o:o + P],
                           "t_cache" if g else None)

            pe.wait_ge(sem("cache"), 32)
            pe.wait_ge(sem("prm_ready"), 3)
            cache_by_channel(0)
            pe.wait_ge(sem("xs"), 6)
            for kk in range(KT):
                wait(pe, "xl", 2 * (kk - 1))
                for c in range(1, 5):
                    tr(out[kk % 2][:, 0, P * (c - 1):P * c], xtok0[:, c, kk * P:kk * P + P])
                tr(out[kk % 2][:, 1, NMETA:P0], xtok0[:, SMP, kk * P:kk * P + P])
                tr(out[kk % 2][:, 1, 0:NMETA], xtok0[0:NMETA, 0, kk * P:kk * P + P], "t_x")
            pe.wait_ge(sem("xl"), 2 * KT - 2)
            gemm(pe, N(0), XH, XL, rhs_ready=lambda kk: kk == KT - 1 and pe.wait_ge(sem("xl"), 2 * KT))
            cache_by_channel(4)
            def columns():
                pe.wait_ge(sem("wld"), 1)
                for c, (c_, L) in enumerate(CHUNKS):
                    for x, rr in enumerate((0, 2, 5)):
                        o = (3 * c + x) * HEADS
                        tr(B4[0:L, o:o + HEADS], row(rr)[:, c_:c_ + L])
                mm(B5[:, 0:52], ones[0:HEADS, :], wld[:, :, :].rearrange("p h j -> p (h j)"))
                tr(B5[0:NB, 64:64 + HEADS], wlr[:, NPC:13], "t_cols")

            def headnorm_out(i):
                pe.wait_ge(sem("hn"), 6 * i + 6)
                pe.wait_ge(sem("c0t_ready"), NB * i + NB)
                pe.wait_ge(sem("hti"), i + 1)
                for x in range(2):
                    for c in range(1, 5):
                        tr((B4, B5)[x][:, P * (c - 1):P * c], num[:, c, x * P:x * P + P])
                for x in range(2):
                    tr(B6[:, x * TS:x * TS + TS], num[:, SMP, x * P:x * P + P], "t_ht" if x else None)
                pe.wait_ge(sem("c1"), NB * i + NB)
                pe.wait_ge(sem("ct_ready"), NPC * i + NPC)
                for e in range(2):
                    for j in range(2):
                        tr(B7[:, e * DH + j * P:e * DH + j * P + P], ct[:, j, e * P:e * P + P],
                           "t_ct" if e and j else None)

            def u_out(i, n):
                evacuated(pe, n + 9)
                evacuated(pe, n + 11)
                pe.wait_ge(sem("hmf"), i + 1)
                pe.wait_ge(sem("cp_sb"), i + 1)
                pe.wait_ge(sem("cache_in"), 32 * (i + 1))
                for g in range(NB // 2):
                    o = PL + 2 * g * WIN + LB
                    for x in range(2):
                        tr((B6, B7)[g // 2][0:UR, (g % 2) * 256 + x * P:(g % 2) * 256 + x * P + P], up[:, x, o:o + UR])
                for x in range(2):
                    tr(B5[0:PAD, x * P:x * P + P], up[:, x, TP:PL], "t_u" if x else None)

            def by_frame(src, bank, pair):
                for c in range(2 * pair, 2 * pair + 2):
                    c_, L = CHUNKS[c]
                    for x in range(2):
                        o = (c % 2) * DH + x * P
                        tr(bank[0:L, o:o + P], src[:, x, c_:c_ + L], "t_kv" if c % 2 and x else None)

            def slot(i, s):
                if s in NUM_SLOT:
                    pe.wait_ge(sem("p_ready"), 6 * i + NUM_SLOT[s] + 1)
                    wait(pe, "num", 6 * i + NUM_SLOT[s])
                if s in TR_SLOT:
                    b = TR_SLOT[s]
                    if b == 0:
                        pe.wait_ge(sem("kv_tok"), 8 * i + 8)
                    wait(pe, "c0t_ready", NB * i + b)
                    pe.wait_ge(sem(f"c0_in{b % C0RING}"), 16 * ((NB // C0RING) * i + b // C0RING + 1))
                    for e in range(2):
                        for j in range(2):
                            tr(B4[:, j * DH + e * P:j * DH + e * P + P], c0[:, b % C0RING, e, j * P:j * P + P],
                               "t_c0" if e and j else None)
                if s in S_SLOT or s in INT_SLOT or NUM_SLOT.get(s, NPC) < NPC:
                    wait(pe, "p_ready", 6 * i + sum(x < s for x in S_SLOT))
                    wait(pe, "ct_ready", NPC * i + sum(x < s and c < NPC for x, c in NUM_SLOT.items()))
                if s in INT_SLOT:
                    b = INT_SLOT[s]
                    pe.wait_ge(sem("c0t_ready"), NB * i + b + 1)
                    if b == 0:
                        pe.wait_ge(sem("qw_ready"), i + 1)
                    for e in range(2):
                        for j in range(2):
                            o = P + e * P + b * LB
                            c_ = NMETA + b * LB
                            ins = mm(B5[:, o:o + LB], c0t[:, j, e * P:e * P + P], qw[:, j, c_:c_ + LB],
                                     j == 0, j == 1)
                    ins.then_inc(sem("t_int"), 1)
                if s in S_SLOT:
                    c = S_SLOT[s]
                    c_, L = CHUNKS[c]
                    if c == 0:
                        pe.wait_ge(sem("kv_tok"), 8 * i + 8)
                    for x in range(2):
                        ins = mm(B5[0:L, 0:L], k[:, x, c_:c_ + L], q[:, x, c_:c_ + L], x == 0, x == 1)
                    ins.then_inc(sem("t_s"), 1)
                if s == 11:
                    pe.wait_ge(sem("num"), 6 * i + NPC)
                    mm(B6[0:NB, 0:DH], wsb[:, :], ktok[:, SMP, :]).then_inc(sem("t_n1"), 1)
                if s in NUM_SLOT:
                    c = NUM_SLOT[s]
                    c_, L = CHUNKS[c]
                    o = B6[0:L, 0:257]
                    if c == 0:
                        ins = mm(o, pt[0:L, 0, 0:L], vtok[0:L, c, :])
                    elif c < NPC:
                        pe.wait_ge(sem("ct_ready"), NPC * i + c)
                        mm(o, pt[0:L, c % 2, 0:L], vtok[0:L, c, :], True, False)
                        for j in range(2):
                            ins = mm(o, qw[:, j, c_:c_ + L], ct[:, j, :], False, j == 1)
                    else:
                        pe.wait_ge(sem("n1"), i + 1)
                        pe.wait_ge(sem("hti"), i + 1)
                        pe.wait_ge(sem("nq"), i + 1)
                        mm(o, pt[:, c % 2, :], vtok[:, c, :], True, False)
                        for e in range(2):
                            mm(B6[:, e * P:e * P + P], hti[:, e, :], ident[:, :], False, False)
                        for j in range(2):
                            ins = mm(B6[:, DH:DH + 1], nqs[:, j, :], onesd[:, :], False, j == 1)
                    ins.then_inc(sem("t_num"), 1)
                for u, (kind, c) in enumerate(UPDATES):
                    if (NUM_SLOT if kind == "U" else UPD_SLOT).get(s) != c:
                        continue
                    pe.wait_ge(sem("vws"), NUPD * i + u + 1)
                    if u:
                        if UPDATES[u - 1][0] == "U":
                            pe.wait_ge(sem("ct_ready"), NPC * i + UPDATES[u - 1][1] + 1)
                        else:
                            pe.wait_ge(sem("c1"), NB * i + UPDATES[u - 1][1] + 1)
                    else:
                        wait(pe, "cp_sb", i)
                    w = vws[:, u % 2, :]
                    if kind == "U":
                        L = CHUNKS[c][1]
                        for j in range(2):
                            mm(B5[:, 384 + j:385 + j], ktok[0:L, c, j * P:j * P + P], w[0:L, DH:DH + 1])
                        for j in range(2):
                            ins = mm(B7[:, j * DH:j * DH + DH], ktok[0:L, c, j * P:j * P + P], w[0:L, 0:DH])
                    else:
                        for e in range(2):
                            ins = mm(B7[:, e * DH:e * DH + DH], w[:, e * P:e * P + P], ktok[:, SMP, :])
                    ins.then_inc(sem("t_upd"), 1)

            def head(i):
                first = isinstance(i, int)
                n = N(N_HEADS0, PER_HEAD, i)
                for r in range(PER_HEAD):
                    if r < 8:
                        gemm(pe, n + r, XH, XL)
                    else:
                        gemm(pe, n + r, XH, XL, gaps=[lambda s=3 * (r - 8) + g: slot(i, s) for g in (1, 2)])
                        slot(i, 3 * (r - 8) + 3)
                    if r == 1 and not first:
                        headnorm_out(i - 1)
                    if r == 2 and not first:
                        u_out(i - 1, n + -PER_HEAD)
                    if r == 4 and first:
                        columns()
                    if r == (5 if first else 3):
                        evacuated(pe, n + 1)
                        if first:
                            pe.wait_ge(sem("cols"), 3)
                        else:
                            pe.wait_ge(sem("hmf"), i)
                            pe.wait_ge(sem("u_sb"), 3 * i)
                        by_frame(k, B4, 0)
                        by_frame(k, B5, 1)
                    if r == (6 if first else 4):
                        pe.wait_ge(sem("kv_tok"), 8 * i + 2)
                        by_frame(k, B4, 2)
                    if r == (7 if first else 6):
                        evacuated(pe, n + 5)
                        pe.wait_ge(sem("kv_tok"), 8 * i + 4)
                        by_frame(vf, B5, 0)
                        by_frame(vf, B4, 1)
                        by_frame(vf, B6, 2)
                    if r == 7:
                        slot(i, 0)
                slot(i, 13)

            head(0)
            with pe.Fori(1, HEADS) as i:
                head(i)
            for j in range(2 * KT):
                if j % 4 < 2:
                    gemm(pe, N(N_GM0 + j), XH2, XL2, gaps=[lambda: headnorm_out(HEADS - 1)] if j == 1 else ())
                else:
                    gemm(pe, N(N_GM0 + j), GH, GL, rhs_ready=(lambda kk: kk == 6 and pe.wait_ge(sem("hm_lo"), HEADS))
                         if j == 2 else None)
                if j == 2:
                    u_out(HEADS - 1, N(N_HEADS0 + PER_HEAD * (HEADS - 1)))

            def channel_sum(acc, b0, b1, name):
                mm(b0[:, :], ones[:, :], acc[:, TS:T2])
                mm(b1[:, 0:TS], ones[:, :], acc[:, 0:TS]).then_inc(sem(name), 1)

            def frame_sums(acc, bank, starts, name):
                for j, c_ in enumerate(starts):
                    ins = mm(bank[:, j:j + 1], acc[:, c_:c_ + P], onesd[:, :])
                ins.then_inc(sem(name), 1)

            def spread(ready, name):
                pe.wait_ge(sem(ready), 1)
                for j in range(5):
                    ins = mm(B6[:, P * j:P * j + P] if j < 4 else B7[:, 0:TS],
                             sm[:, 6 + j:7 + j].to_broadcast([P, P]), ident[:, :])
                ins.then_inc(sem(name), 1)

            for r in range(KT):
                gemm(pe, N(N_GC0 + r), XH2, XL2, gaps=[lambda: spread("lrt", "t_lr")] if r == 5 else ())
                if r == 1:
                    pe.wait_ge(sem("lsum"), 1)
                    channel_sum(ln[0], B4, B5, "t_ln")
                if r == 4:
                    pe.wait_ge(sem("lsq"), KT)
                    pe.wait_ge(sem("mean"), 2)
                    frame_sums(ln[4], B4, OUTC, "t_ln")
            for r in range(KT):
                gemm(pe, N(N_GC0 + KT + r), GH, GL,
                     rhs_ready=(lambda kk: pe.wait_ge(sem("cl"), kk + 1)) if r == 0 else None)
            for r in range(KT):
                gemm(pe, N(N_OUT0 + r), XH2, XL2,
                     rhs_ready=(lambda kk: pe.wait_ge(sem("ml"), kk + 1)) if r == 0 else None)
                if r == 1:
                    for c in range(1, 6):
                        pe.wait_ge(sem(f"xagain{c}"), 16)
                for x in [0, 1] if r == 1 else [r] if r else []:
                    b0, b1 = (B4, B5) if x % 2 == 0 else (B6, B7)
                    wait(pe, "xa", 2 * (x - 1))
                    for c in range(1, 5):
                        tr(b0[:, P * (c - 1):P * c], xtok5[:, c, x * P:x * P + P])
                    tr(b1[:, 0:TS], xtok5[:, SMP, x * P:x * P + P], "t_xa")
            pe.wait_ge(sem("oacc"), KT)
            pe.wait_ge(sem("xa"), 2 * KT)
            frame_sums(tmp[6], B4, OUTC, "t_os")
            spread("ort", "t_or")

            def by_frames(src, b0, b1, name):
                for j, c_ in enumerate(OUTC):
                    tr(b0[:, P * j:P * j + P] if j < 4 else b1[:, 0:P], src[:, c_:c_ + P], name if j == 4 else None)

            def ffn(c, last=False):
                n = N(N_FF0, 2 * KT, c)
                if last:
                    pe.wait_ge(sem("fsum"), 2 * KT - 1)
                    frame_sums(tmp[7], B5, OUTC, "t_fs")
                for r in range(KT):
                    gemm(pe, n + r, XH2, XL2, rhs_ready=(lambda kk: pe.wait_ge(sem("fl"), kk + 1)) if r == 0 else None)
                    if last:
                        wait(pe, "x2t", 2 * r)
                        by_frames(MG[:, r, :], B6, B7, "t_x2")
                for r in range(KT):
                    gemm(pe, n + (KT + r), GH, GL,
                         rhs_ready=(lambda kk: pe.wait_ge(sem("hl"), c * KT + (kk + 1))) if r == 0 else None)
                    if last and r:
                        y_frames(r - 1)

            def y_frames(r):
                pe.wait_ge(sem("yg"), r + 1)
                wait(pe, "yt", 2 * r)
                by_frames(CV[:, r, :], B4, B5, "t_y")

            with pe.Fori(0, DFF // D - 1) as c:
                ffn(c)
            ffn(DFF // D - 1, last=True)
            pe.wait_ge(sem("yacc"), KT)
            pe.wait_ge(sem("x2t"), 2 * KT)
            frame_sums(tmp[6], B7, OUTC, "t_ys")
            y_frames(KT - 1)


_INS = ["x_prompt", "x_sample", "state_mlstm_C", "state_mlstm_n", "state_mlstm_m", "cache_conv", "meta_tokens",
        "g_pre_mix", "w_in", "b_if", "g_headnorm", "w_branch_m", "conv_w", "conv_b", "ln_g", "ln_b", "w_branch_c",
        "w_out", "g_post_mix", "g_pre_ffn", "w_ff1", "w_ff2", "g_post_ffn"]
_OUTS = [("o_y_prompt", (1, SEQ, D)), ("o_y_sample", (NB, LB, D)), ("o_C_prompt", (1, 1, HEADS, DH, DH)),
         ("o_n_prompt", (1, 1, HEADS, DH)), ("o_m_prompt", (1, 1, HEADS)), ("o_conv_prompt", (1, 1, PAD, D)),
         ("o_C_sample", (1, NB, HEADS, DH, DH)), ("o_n_sample", (1, NB, HEADS, DH)), ("o_m_sample", (1, NB, HEADS)),
         ("o_conv_sample", (1, NB, PAD, D))]


def kernel(**inputs):
    import concourse.bacc as bacc
    from concourse.bass_utils import run_bass_kernel_spmd

    nc = bacc.Bacc("TRN2", target_bir_lowering=False, num_devices=1)
    arrays, aps = {}, {}
    for name in _INS:
        x = np.ascontiguousarray(inputs[name])
        arrays["in_" + name] = x
        aps[name] = nc.dram_tensor("in_" + name, x.shape, mybir.dt.from_np(x.dtype), kind="ExternalInput").ap()
    for name, shape in _OUTS:
        aps[name] = nc.dram_tensor(name, shape, F32, kind="ExternalOutput").ap()
    build(nc, aps)
    r = run_bass_kernel_spmd(nc, [arrays], core_ids=[0])
    return tuple(r.results[0][name] for name, _ in _OUTS)
```
